# Optimizing a Trainium2 kernel written in Bass

```python
import math
import jax, jax.numpy as jnp
from jax import lax
import numpy as np

D_MODEL = 1024
BATCH = 1
SEQ = 512
DEPTH = 2
DEC_BATCH = 8
DEC_SEQ = 8
PAST_LEN = 512
PAGE_SIZE = 128

N_A_LAYERS = DEPTH // 2
N_B_LAYERS = DEPTH - N_A_LAYERS
DN_ALPHA = (2.0 * DEPTH) ** 0.25
DN_BETA = (8.0 * DEPTH) ** -0.25
LN_EPS = 1e-5
RMS_EPS = 1e-5
D_FF = 4 * D_MODEL

M_D_INNER = 2 * D_MODEL
M_HEAD_DIM = 64
M_N_HEADS = M_D_INNER // M_HEAD_DIM
M_N_GROUPS = 4
M_HPG = M_N_HEADS // M_N_GROUPS
M_D_STATE = 128
M_CONV = 4
M_CHUNK = 128
M_CONV_DIM = M_D_INNER + 2 * M_N_GROUPS * M_D_STATE
M_IN_DIM = M_D_INNER + M_CONV_DIM + M_N_HEADS

A_HEAD_DIM = 64
A_N_HEADS = D_MODEL // A_HEAD_DIM
A_N_KV = 4
A_GROUP = A_N_HEADS // A_N_KV
A_Q_DIM = A_N_HEADS * A_HEAD_DIM
CMP_LEN = 32
CMP_STRIDE = 16
CMP_RATIO = CMP_LEN // CMP_STRIDE
CMP_HIDDEN = 2 * A_HEAD_DIM
SEL_BLOCK = 64
SEL_TOPN = 16
WINDOW = 512
Q_BLOCK = 128
N_BUCKETS = 32
MAX_DISTANCE = 128
MASK_VALUE = -1e30
FORCE_SCORE = 1e3

kernel_name = "yoco_mamba2_nsa_decoder_step"

def layer_norm(x, g, b):
    xf = x.astype(jnp.float32)
    mu = jnp.mean(xf, axis=-1, keepdims=True)
    var = jnp.mean(jnp.square(xf - mu), axis=-1, keepdims=True)
    return ((xf - mu) * lax.rsqrt(var + LN_EPS)).astype(x.dtype) * g + b

def sq_relu_mlp(x, w1, w2):
    return jnp.square(jax.nn.relu(x @ w1)) @ w2

def rel_bucket(dist):
    n = jnp.maximum(dist, 0)
    max_exact = N_BUCKETS // 2
    large = max_exact + (jnp.log(jnp.maximum(n, max_exact).astype(jnp.float32) / max_exact)
                         / math.log(MAX_DISTANCE / max_exact) * (N_BUCKETS - max_exact)).astype(jnp.int32)
    return jnp.where(n < max_exact, n, jnp.minimum(large, N_BUCKETS - 1))

def causal_conv(xbc, conv_state, w, b):
    L = xbc.shape[1]
    xp = jnp.concatenate([conv_state, xbc], axis=1)
    acc = b + xp[:, 0:L] * w[0]
    for k in range(1, M_CONV):
        acc = acc + xp[:, k:k + L] * w[k]
    return jax.nn.silu(acc), xp[:, L:]

def segsum(a):
    T = a.shape[-1]
    aa = jnp.broadcast_to(a[..., :, None], a.shape + (T,))
    aa = jnp.where(jnp.tril(jnp.ones((T, T), bool), -1), aa, 0.0)
    s = jnp.cumsum(aa, axis=-2)
    return jnp.where(jnp.tril(jnp.ones((T, T), bool)), s, -jnp.inf)

def ssd_scan(x, a, Bm, Cm, h0):
    Bn, L, G, R, P = x.shape
    Q = M_CHUNK if L % M_CHUNK == 0 else L
    c = L // Q
    x = x.reshape(Bn, c, Q, G, R, P)
    Bm = Bm.reshape(Bn, c, Q, G, -1)
    Cm = Cm.reshape(Bn, c, Q, G, -1)
    a = a.reshape(Bn, c, Q, G, R).transpose(0, 3, 4, 1, 2)
    a_cum = jnp.cumsum(a, axis=-1)
    lmat = jnp.exp(segsum(a))
    y_diag = jnp.einsum('bclgn,bcsgn,bgrcls,bcsgrp->bclgrp', Cm, Bm, lmat, x)
    decay_states = jnp.exp(a_cum[..., -1:] - a_cum)
    states = jnp.einsum('bclgn,bgrcl,bclgrp->bcgrpn', Bm, decay_states, x)
    states = jnp.concatenate([h0[:, None], states], axis=1)
    chunk_a = jnp.pad(a_cum[..., -1], ((0, 0), (0, 0), (0, 0), (1, 0)))
    decay_chunk = jnp.exp(segsum(chunk_a))
    states = jnp.einsum('bgrzc,bcgrpn->bzgrpn', decay_chunk, states)
    prev_states, h_last = states[:, :-1], states[:, -1]
    y_off = jnp.einsum('bclgn,bcgrpn,bgrcl->bclgrp', Cm, prev_states, jnp.exp(a_cum))
    return (y_diag + y_off).reshape(Bn, L, G, R, P), h_last

def mamba_mixer(h, ssm_state, conv_state, in_w, conv_w, conv_b, dt_bias, a_log, d_skip, norm_w, out_w):
    Bn, L, _ = h.shape
    f32 = jnp.float32
    zxbcdt = h @ in_w
    z, xbc, dt = jnp.split(zxbcdt, [M_D_INNER, M_D_INNER + M_CONV_DIM], axis=-1)
    xbc, new_conv = causal_conv(xbc, conv_state, conv_w, conv_b)
    xs, Bm, Cm = jnp.split(xbc, [M_D_INNER, M_D_INNER + M_N_GROUPS * M_D_STATE], axis=-1)
    xs = xs.reshape(Bn, L, M_N_GROUPS, M_HPG, M_HEAD_DIM).astype(f32)
    Bm = Bm.reshape(Bn, L, M_N_GROUPS, M_D_STATE).astype(f32)
    Cm = Cm.reshape(Bn, L, M_N_GROUPS, M_D_STATE).astype(f32)
    dt = jax.nn.softplus(dt.astype(f32) + dt_bias.astype(f32)).reshape(Bn, L, M_N_GROUPS, M_HPG)
    A = -jnp.exp(a_log.astype(f32)).reshape(M_N_GROUPS, M_HPG)
    h0 = ssm_state.astype(f32).reshape(Bn, M_N_GROUPS, M_HPG, M_HEAD_DIM, M_D_STATE)
    y, h_last = ssd_scan(xs * dt[..., None], dt * A, Bm, Cm, h0)
    y = y + xs * d_skip.astype(f32).reshape(M_N_GROUPS, M_HPG)[:, :, None]
    y = y.reshape(Bn, L, M_D_INNER) * jax.nn.silu(z.astype(f32))
    yg = y.reshape(Bn, L, M_N_GROUPS, M_D_INNER // M_N_GROUPS)
    yg = yg * lax.rsqrt(jnp.mean(yg * yg, axis=-1, keepdims=True) + RMS_EPS)
    y = (yg.reshape(Bn, L, M_D_INNER) * norm_w).astype(h.dtype)
    new_ssm = h_last.reshape(Bn, M_N_HEADS, M_HEAD_DIM, M_D_STATE).astype(ssm_state.dtype)
    return y @ out_w, new_ssm, new_conv

def compress_tokens(tok, w1, pe, w2):
    Bn, T = tok.shape[:2]
    n_chunks = T // CMP_STRIDE
    n_cmp = n_chunks - CMP_RATIO + 1
    chunks = tok[:, :n_chunks * CMP_STRIDE].reshape(Bn, n_chunks, CMP_STRIDE, A_N_KV, A_HEAD_DIM)
    hid = jnp.einsum('bcjgd,jde->bcge', chunks[:, 0:n_cmp] + pe[0:CMP_STRIDE][:, None, :], w1[0])
    for r in range(1, CMP_RATIO):
        part = chunks[:, r:r + n_cmp] + pe[r * CMP_STRIDE:(r + 1) * CMP_STRIDE][:, None, :]
        hid = hid + jnp.einsum('bcjgd,jde->bcge', part, w1[r])
    return jnp.einsum('bcge,ed->bcgd', jax.nn.silu(hid), w2)

def to_sel_blocks(tok):
    Bn, T = tok.shape[:2]
    n_sel = -(-T // SEL_BLOCK)
    tok = jnp.pad(tok, ((0, 0), (0, n_sel * SEL_BLOCK - T), (0, 0), (0, 0)))
    return tok.reshape(Bn, n_sel, SEL_BLOCK, A_N_KV, A_HEAD_DIM)

def shared_kv(h, start, past_cmp, past_sel, past_win, kv_w, cmp_w1, cmp_pe, cmp_w2):
    Bn, Sq, _ = h.shape
    kv = (h @ kv_w).reshape(Bn, Sq, 3, 2, A_N_KV, A_HEAD_DIM)
    new_cmp, new_sel, new_win = kv[:, :, 0], kv[:, :, 1], kv[:, :, 2]
    full_cmp = jnp.concatenate([past_cmp, new_cmp], axis=1)
    full_sel = jnp.concatenate([past_sel, new_sel], axis=1)
    win_rows = jnp.concatenate([past_win, new_win], axis=1)
    n_past_w = past_win.shape[1]
    n_pad = WINDOW - n_past_w
    win_full = jnp.pad(win_rows, ((0, 0), (n_pad, 0), (0, 0), (0, 0), (0, 0)))
    win_pos = jnp.concatenate([jnp.full((n_pad,), -1, jnp.int32),
                               jnp.arange(start - n_past_w, start + Sq, dtype=jnp.int32)])
    k_cmp = compress_tokens(full_cmp[:, :, 0], cmp_w1[0], cmp_pe[0], cmp_w2[0])
    v_cmp = compress_tokens(full_cmp[:, :, 1], cmp_w1[1], cmp_pe[1], cmp_w2[1])
    shared = (k_cmp, v_cmp, to_sel_blocks(full_sel[:, :, 0]), to_sel_blocks(full_sel[:, :, 1]),
              win_full[:, :, 0], win_full[:, :, 1])
    n_keep = min(WINDOW, win_rows.shape[1])
    return shared, win_pos, new_cmp, new_sel, win_rows[:, win_rows.shape[1] - n_keep:]

def softmax_masked(s, mask):
    p = jax.nn.softmax(jnp.where(mask, s, MASK_VALUE), axis=-1)
    return jnp.where(mask, p, 0.0)

def nsa_attend(q, gates, q_pos, shared, win_pos, rel_bias):
    k_cmp, v_cmp, k_sel, v_sel, k_win, v_win = shared
    f32 = jnp.float32
    Bn, Sq = q.shape[:2]
    n_cmp, n_sel = k_cmp.shape[1], k_sel.shape[1]
    qb = Q_BLOCK if Sq % Q_BLOCK == 0 else Sq
    nqb = Sq // qb
    top_n = min(SEL_TOPN, n_sel)
    win_len = WINDOW + qb
    scale = A_HEAD_DIM ** -0.5
    cmp_start = jnp.arange(n_cmp, dtype=jnp.int32) * CMP_STRIDE
    cmp_end = cmp_start + CMP_LEN - 1
    sel_start = jnp.arange(n_sel, dtype=jnp.int32) * SEL_BLOCK
    sel_idx = jnp.arange(n_sel, dtype=jnp.int32)
    overlap = ((cmp_start[:, None] < sel_start[None, :] + SEL_BLOCK)
               & (cmp_start[:, None] + CMP_LEN > sel_start[None, :])).astype(f32)
    bias_hgr = rel_bias.astype(f32).reshape(N_BUCKETS, A_N_KV, A_GROUP)
    bias_g = bias_hgr.transpose(1, 0, 2)
    g_idx = jnp.arange(A_N_KV)

    def per_block(args, kc, vc, ksg, vsg, kw, vw):
        qq, gg, pos, s0 = args
        s_c = jnp.einsum('qgrd,cgd->qgrc', qq, kc).astype(f32) * scale
        s_c = s_c + bias_hgr[rel_bucket(pos[:, None] - cmp_end[None, :])].transpose(0, 2, 3, 1)
        m_c = (cmp_end[None, :] <= pos[:, None])[:, None, None, :]
        p_c = softmax_masked(s_c, m_c)
        o_c = jnp.einsum('qgrc,cgd->qgrd', p_c.astype(vc.dtype), vc)
        imp = jnp.einsum('qgrc,cs->qgs', p_c, overlap)
        blk = pos // SEL_BLOCK
        valid = sel_start[None, :] <= pos[:, None]
        forced = (sel_idx[None, :] == 0) | (sel_idx[None, :] == blk[:, None]) | (sel_idx[None, :] == blk[:, None] - 1)
        score = jnp.where(valid[:, None, :], imp + jnp.where(forced, FORCE_SCORE, 0.0)[:, None, :], -1.0)
        _, idx = lax.top_k(score, top_n)
        kg = ksg[g_idx[None, :, None], idx]
        vg = vsg[g_idx[None, :, None], idx]
        k_pos = idx[..., None] * SEL_BLOCK + jnp.arange(SEL_BLOCK, dtype=jnp.int32)
        s_s = jnp.einsum('qgrd,qgkld->qgrkl', qq, kg).astype(f32) * scale
        b_s = bias_g[g_idx[None, :, None, None], rel_bucket(pos[:, None, None, None] - k_pos)]
        s_s = s_s + b_s.transpose(0, 1, 4, 2, 3)
        m_s = (k_pos <= pos[:, None, None, None])[:, :, None]
        p_s = softmax_masked(s_s.reshape(qb, A_N_KV, A_GROUP, -1), m_s.reshape(qb, A_N_KV, 1, -1))
        o_s = jnp.einsum('qgrm,qgmd->qgrd', p_s.astype(vg.dtype), vg.reshape(qb, A_N_KV, -1, A_HEAD_DIM))
        kwb = lax.dynamic_slice_in_dim(kw, s0, win_len, axis=0)
        vwb = lax.dynamic_slice_in_dim(vw, s0, win_len, axis=0)
        wpos = lax.dynamic_slice_in_dim(win_pos, s0, win_len, axis=0)
        dist = pos[:, None] - wpos[None, :]
        s_w = jnp.einsum('qgrd,kgd->qgrk', qq, kwb).astype(f32) * scale
        s_w = s_w + bias_hgr[rel_bucket(dist)].transpose(0, 2, 3, 1)
        m_w = ((wpos[None, :] >= 0) & (dist >= 0) & (dist < WINDOW))[:, None, None, :]
        p_w = softmax_masked(s_w, m_w)
        o_w = jnp.einsum('qgrk,kgd->qgrd', p_w.astype(vwb.dtype), vwb)
        gf = gg.astype(f32)
        o = gf[..., 0:1] * o_c + gf[..., 1:2] * o_s + gf[..., 2:3] * o_w
        return o.reshape(qb, A_Q_DIM).astype(qq.dtype)

    def per_seq(args):
        qs, gs, kc, vc, ks, vs, kw, vw = args
        ksg = ks.transpose(2, 0, 1, 3)
        vsg = vs.transpose(2, 0, 1, 3)
        blocks = (qs.reshape(nqb, qb, A_N_KV, A_GROUP, A_HEAD_DIM),
                  gs.reshape(nqb, qb, A_N_KV, A_GROUP, 3),
                  q_pos.reshape(nqb, qb),
                  jnp.arange(nqb, dtype=jnp.int32) * qb)
        out = lax.map(lambda a: per_block(a, kc, vc, ksg, vsg, kw, vw), blocks)
        return out.reshape(Sq, A_Q_DIM)

    return lax.map(per_seq, (q, gates, k_cmp, v_cmp, k_sel, v_sel, k_win, v_win))

def nsa_mixer(h, q_pos, shared, win_pos, qg_w, o_w, rel_bias):
    Bn, Sq, _ = h.shape
    qg = h @ qg_w
    q = qg[..., :A_Q_DIM].reshape(Bn, Sq, A_N_HEADS, A_HEAD_DIM)
    gates = jax.nn.sigmoid(qg[..., A_Q_DIM:].astype(jnp.float32)).reshape(Bn, Sq, A_N_HEADS, 3)
    o = nsa_attend(q, gates, q_pos, shared, win_pos, rel_bias)
    return o @ o_w

def run_group(x, start, ssm0, conv0, past_cmp, past_sel, past_win, weights):
    (ln_g, ln_b, m_in_w, m_conv_w, m_conv_b, m_dt_bias, m_a_log, m_d, m_norm_w, m_out_w,
     kv_w, cmp_w1, cmp_pe, cmp_w2, q_w, o_w, rel_bias, mlp_w1, mlp_w2) = weights
    Bn, Sq, _ = x.shape
    q_pos = start + jnp.arange(Sq, dtype=jnp.int32)
    h = x
    new_ssm, new_conv = [], []
    for i in range(DEPTH):
        if i < N_A_LAYERS:
            mix, s_i, c_i = mamba_mixer(h, ssm0[i], conv0[i], m_in_w[i], m_conv_w[i], m_conv_b[i],
                                        m_dt_bias[i], m_a_log[i], m_d[i], m_norm_w[i], m_out_w[i])
            new_ssm.append(s_i)
            new_conv.append(c_i)
        else:
            if i == N_A_LAYERS:
                shared, win_pos, new_cmp, new_sel, new_win = shared_kv(
                    h, start, past_cmp, past_sel, past_win, kv_w, cmp_w1, cmp_pe, cmp_w2)
            j = i - N_A_LAYERS
            mix = nsa_mixer(h, q_pos, shared, win_pos, q_w[j], o_w[j], rel_bias)
        h = layer_norm(DN_ALPHA * h + mix, ln_g[i, 0], ln_b[i, 0])
        h = layer_norm(DN_ALPHA * h + sq_relu_mlp(h, mlp_w1[i], mlp_w2[i]), ln_g[i, 1], ln_b[i, 1])
    return h, jnp.stack(new_ssm), jnp.stack(new_conv), new_cmp, new_sel, new_win

def setup_inputs(seed: int = 0) -> dict:
    key = jax.random.key(seed)
    ks = jax.random.split(key, 28)
    f32 = jnp.float32

    def nrm(k, shape, scale):
        return jax.random.normal(k, shape, f32) * scale

    n_pages = PAST_LEN // PAGE_SIZE
    n_used = DEC_BATCH * n_pages
    n_phys = n_used + n_used // 4
    win_keep = min(WINDOW, PAST_LEN)
    kv_row = (2, A_N_KV, A_HEAD_DIM)
    page_table = jax.random.permutation(ks[7], n_phys)[:n_used].reshape(DEC_BATCH, n_pages).astype(jnp.int32)
    dt0 = jnp.exp(jax.random.uniform(ks[13], (N_A_LAYERS, M_N_HEADS), f32, math.log(1e-3), math.log(1e-1)))
    return {
        "x_prompt": nrm(ks[0], (BATCH, SEQ, D_MODEL), 1.0),
        "x_sample": nrm(ks[1], (DEC_BATCH, DEC_SEQ, D_MODEL), 1.0),
        "state_ssm": nrm(ks[2], (N_A_LAYERS, DEC_BATCH, M_N_HEADS, M_HEAD_DIM, M_D_STATE), 0.1),
        "state_conv": nrm(ks[3], (N_A_LAYERS, DEC_BATCH, M_CONV - 1, M_CONV_DIM), 1.0),
        "cache_cmp_kv": nrm(ks[4], (n_phys, PAGE_SIZE) + kv_row, 1.0),
        "cache_sel_kv": nrm(ks[5], (n_phys, PAGE_SIZE) + kv_row, 1.0),
        "cache_win_kv": nrm(ks[6], (DEC_BATCH, win_keep) + kv_row, 1.0),
        "page_table": page_table,
        "ln_g": 1.0 + nrm(ks[8], (DEPTH, 2, D_MODEL), 0.05),
        "ln_b": nrm(ks[9], (DEPTH, 2, D_MODEL), 0.02),
        "m_in_w": nrm(ks[10], (N_A_LAYERS, D_MODEL, M_IN_DIM), D_MODEL ** -0.5),
        "m_conv_w": nrm(ks[11], (N_A_LAYERS, M_CONV, M_CONV_DIM), M_CONV ** -0.5),
        "m_conv_b": nrm(ks[12], (N_A_LAYERS, M_CONV_DIM), 0.02),
        "m_dt_bias": dt0 + jnp.log(-jnp.expm1(-dt0)),
        "m_a_log": jnp.log(jax.random.uniform(ks[14], (N_A_LAYERS, M_N_HEADS), f32, 1.0, 16.0)),
        "m_d": 1.0 + nrm(ks[15], (N_A_LAYERS, M_N_HEADS), 0.1),
        "m_norm_w": 1.0 + nrm(ks[16], (N_A_LAYERS, M_D_INNER), 0.05),
        "m_out_w": nrm(ks[17], (N_A_LAYERS, M_D_INNER, D_MODEL), M_D_INNER ** -0.5 * DN_BETA),
        "kv_w": nrm(ks[18], (D_MODEL, 3 * 2 * A_N_KV * A_HEAD_DIM), D_MODEL ** -0.5),
        "cmp_w1": nrm(ks[19], (2, CMP_RATIO, CMP_STRIDE, A_HEAD_DIM, CMP_HIDDEN), (CMP_LEN * A_HEAD_DIM) ** -0.5),
        "cmp_pe": nrm(ks[20], (2, CMP_LEN, A_HEAD_DIM), 0.5),
        "cmp_w2": nrm(ks[21], (2, CMP_HIDDEN, A_HEAD_DIM), CMP_HIDDEN ** -0.5),
        "q_w": nrm(ks[22], (N_B_LAYERS, D_MODEL, A_Q_DIM + 3 * A_N_HEADS), D_MODEL ** -0.5),
        "o_w": nrm(ks[23], (N_B_LAYERS, A_Q_DIM, D_MODEL), A_Q_DIM ** -0.5 * DN_BETA),
        "rel_bias": nrm(ks[24], (N_BUCKETS, A_N_HEADS), 0.5),
        "mlp_w1": nrm(ks[25], (DEPTH, D_MODEL, D_FF), D_MODEL ** -0.5),
        "mlp_w2": nrm(ks[26], (DEPTH, D_FF, D_MODEL), D_FF ** -0.5 * DN_BETA),
    }

def reference(x_prompt, x_sample, state_ssm, state_conv, cache_cmp_kv, cache_sel_kv, cache_win_kv, page_table,
              ln_g, ln_b, m_in_w, m_conv_w, m_conv_b, m_dt_bias, m_a_log, m_d, m_norm_w, m_out_w,
              kv_w, cmp_w1, cmp_pe, cmp_w2, q_w, o_w, rel_bias, mlp_w1, mlp_w2):
    weights = (ln_g, ln_b, m_in_w, m_conv_w, m_conv_b, m_dt_bias, m_a_log, m_d, m_norm_w, m_out_w,
               kv_w, cmp_w1, cmp_pe, cmp_w2, q_w, o_w, rel_bias, mlp_w1, mlp_w2)
    kv_row = (2, A_N_KV, A_HEAD_DIM)
    empty_kv = jnp.zeros((BATCH, 0) + kv_row, cache_cmp_kv.dtype)
    y_prompt, p_ssm, p_conv, p_cmp, p_sel, p_win = run_group(
        x_prompt, 0,
        jnp.zeros((N_A_LAYERS, BATCH, M_N_HEADS, M_HEAD_DIM, M_D_STATE), state_ssm.dtype),
        jnp.zeros((N_A_LAYERS, BATCH, M_CONV - 1, M_CONV_DIM), state_conv.dtype),
        empty_kv, empty_kv, jnp.zeros((BATCH, 0) + kv_row, cache_win_kv.dtype), weights)
    n_pages = PAST_LEN // PAGE_SIZE
    past_cmp = cache_cmp_kv[page_table].reshape((DEC_BATCH, n_pages * PAGE_SIZE) + kv_row)
    past_sel = cache_sel_kv[page_table].reshape((DEC_BATCH, n_pages * PAGE_SIZE) + kv_row)
    y_sample, s_ssm, s_conv, s_cmp, s_sel, s_win = run_group(
        x_sample, PAST_LEN, state_ssm, state_conv, past_cmp, past_sel, cache_win_kv, weights)
    return (y_prompt, y_sample, p_ssm, p_conv, p_cmp, p_sel, p_win, s_ssm, s_conv, s_cmp, s_sel, s_win)


_drawn_inputs = setup_inputs


def setup_inputs(seed=0):
    import zlib

    import numpy as np

    out = dict(_drawn_inputs(seed))
    spreads = {}
    factors = {'cache_sel_kv': 3.772, 'm_d': 3.411, 'm_norm_w': 3.298}
    for name, (base, spread) in spreads.items():
        noise = np.random.default_rng([zlib.crc32(name.encode()), seed]).standard_normal(out[name].shape)
        drawn = base * np.exp(spread * noise) if base else spread * noise
        out[name] = __import__('jax').numpy.asarray(drawn.astype(out[name].dtype))
    for name, factor in factors.items():
        out[name] = (out[name] * factor).astype(out[name].dtype)
    return out
```

```python
from contextlib import ExitStack

import numpy as np

import concourse.bass as bass
from concourse import mybir

F32 = mybir.dt.float32
I32 = mybir.dt.int32
ALU = mybir.AluOpType
ACT = mybir.ActivationFunctionType
AX = mybir.AxisListType

P = 128
D = 1024
KC = D // P
NP_TOK = 512
NB, NS = 8, 8
ND = NB * NS
T = NP_TOK + ND
PAST = 512
PAGE = 128
NPG = PAST // PAGE
NPHYS = NB * NPG + NB * NPG // 4
DI = 2 * D
MH, MP, MN, MG = 32, 64, 128, 4
HPG = MH // MG
GB = 10
XB = 6
NXB = MG * XB
CONV = 4
NH, NKV, HD = 16, 4, 64
GR = NH // NKV
DFF = 4 * D
NBK = 32
NCMP = 32
CL, CS = 32, 16
ALPHA = 4.0 ** 0.25
LN_EPS = 1e-5
RMS_EPS = 1e-5
SCALE = float(HD) ** -0.5
NEG = -1e30
Y0 = 527
X0 = 527
CB0 = 353
NSIG = 56
XN = 1040
ARENA = 41500
SLOT = KC * P
NSLOT = 4
NT = 5
RB = 256
RW = 384

SL_IN = MG * GB
SL_OUT = KC * 2
SL_M1 = DFF // P
SL_M2 = KC * 4
SL_KV = 12
SL_Q = 8
SL_O = 8
N_SLOTS = SL_IN + SL_OUT + SL_M1 + SL_M2 + SL_KV + SL_Q + SL_O + SL_M1 + SL_M2


def build(nc, a):
    with ExitStack() as ctx:
        def sb(name, shape, dt=F32):
            return ctx.enter_context(nc.sbuf_tensor(name, shape, dt))

        def sem(name):
            return ctx.enter_context(nc.semaphore(name))

        bD = [ctx.enter_context(nc.psum_tensor(f"bD{i}", [P, 512], F32)) for i in range(2)]
        bDn = ctx.enter_context(nc.psum_tensor("bDn", [P, 2, 512], F32))
        bX = ctx.enter_context(nc.psum_tensor("bX", [P, 512], F32))
        bM = ctx.enter_context(nc.psum_tensor("bM", [P, 512], F32))
        bS = ctx.enter_context(nc.psum_tensor("bS", [P, 2, 512], F32))

        xT = sb("xT", [P, KC, T])
        ring = sb("ring", [P, NSLOT, SLOT])
        ident = sb("ident", [P, P])
        triu = sb("triu", [P, 2, P])
        low = sb("low", [P, 2, P])
        ones = sb("ones", [P, P])
        onesd = sb("onesd", [P, P])
        lng = sb("lng", [P, 4, KC])
        lnb = sb("lnb", [P, 4, KC])
        row = sb("row", [P, T])
        sq = sb("sq", [P, 2, T])
        arena = sb("arena", [P, ARENA])
        at = [0]

        def carve(*shape, parts=P):
            n = int(np.prod(shape))
            v = arena[0:parts, at[0]:at[0] + n]
            at[0] += n
            assert at[0] <= ARENA, at[0]
            if len(shape) == 1:
                return v
            names = "abcd"[:len(shape)]
            return v.rearrange(f"p ({' '.join(names)}) -> p {' '.join(names)}",
                               **{k: s for k, s in zip(names[1:], shape[1:])})

        y = carve(DI // P, T)
        xbc = [carve(XB, T) for _ in range(2)]
        raw = [carve(3 + NP_TOK + NB * (3 + NS)) for _ in range(2)]
        acc = [carve(T) for _ in range(2)]
        cst = carve(NXB, NB, 3)
        lastp = carve(NXB, 3)
        lastd = carve(NXB, NB, 3)
        cw = carve(NXB, CONV)
        cb = carve(NXB)
        nw = carve(DI // P)
        dsk = carve(DI // P)
        dtw = carve(KC, MH)
        dtb = carve(2, parts=MH)
        smask = carve(NB, parts=ND)
        dtT = carve(T, parts=MH)
        dw = [carve(T, parts=MH) for _ in range(4)]
        aT = carve(T, parts=MH)
        dt_tok = carve(NT, MH)
        a_tok = carve(NT, MH)
        dec_tok = carve(NT, MH)
        tot = carve(4, MH)
        totd = carve(NB, MH)
        am = carve(NB, MH, parts=ND)
        AH = carve(HPG, P)
        AR = carve(HPG * MP)
        Lm = carve(HPG, P)
        Gm = carve(P)
        E = carve(512)
        xdt = carve(HPG * MP)
        xdec = carve(HPG * MP)
        Btok = carve(P)
        Bm = carve(NB, P, parts=ND)
        st = carve(MG, HPG * MP)
        tmp = [carve(HPG * MP) for _ in range(2)]
        yt = carve(512)
        sdec = carve(NB, HPG * MP)
        mamba_end = at[0]

        at[0] = 0
        hid = carve(DFF // P, T)
        hid_end = at[0]

        at[0] = 0
        kvT = carve(12, T)
        qT = carve(8, T)
        qn = carve(2, NB, GR * NS)
        Vt = carve(NT, 2, NKV, HD)
        kc = carve(NB + 1, 2, NCMP)
        vc = carve(NB + 1, NKV, HD, parts=NCMP)
        gates = carve(NT, 3 * NH)
        gn = carve(NB, 3)
        mx, nmx, sm, wt = carve(2, 4), carve(2, 4), carve(2, 4), carve(2, 4)
        SB = [bD[0], bD[1], bS[:, 0, :], bS[:, 1, :]]
        cmx, csm = carve(NH), carve(NH)
        dmx, dnm, dsm, dwt = carve(5), carve(3), carve(3), carve(3)
        assert at[0] <= hid_end
        at[0] = hid_end
        ct = [carve(NPG, 512) for _ in range(2)]
        cw1 = carve(2, 2, 8, P)
        at[0] = hid_end
        skv = [carve(NPG, 512) for _ in range(2)]
        wkv = [carve(NPG, 512) for _ in range(2)]
        relb = carve(NH, parts=NBK + 1)
        cw2 = carve(2, HD)
        cpe = carve(2, 2, 8)
        hpe = carve(2)
        h1s = [carve(NKV, NCMP + 1) for _ in range(2)]
        hs = [carve(NKV, NCMP) for _ in range(2)]
        gw = carve(KC, 3 * NH)
        cbt = carve(NSIG, NH)
        cvalid = carve(4)
        bd = carve(512)
        bdw = carve(512)
        bdn = carve(NB * 72)
        bdc = carve(NCMP)
        FARC = (PAST - P - CL + 1) // CS + 1
        nr = carve(P + NS * 2)
        wmask = carve(NS)
        Pc = carve(NH, NCMP)
        Rs = carve(NH, RB)
        b0 = at[0]
        Pb = [carve(GR, NP_TOK) for _ in range(2)]
        PT = [carve(512) for _ in range(4)]
        at[0] = b0
        ef = carve(XN, parts=NBK + 1)
        eb = carve(XN, parts=NBK + 1)
        bt = carve(XN, parts=NH)
        at[0] = b0 + 2048
        zx = carve(4, 256)
        at[0] = b0 + 4096
        tp = carve(2, NKV, 8, NCMP)
        at[0] = b0
        Pd = [carve(2 * (PAST + ND) + NCMP) for _ in range(2)]
        PTd = carve(2 * PAST)
        PTs = carve(3 * P)
        ptab = sb("ptab", [1, NB * NPG], I32)

        S_OUT = SL_IN
        S_M1 = [S_OUT + SL_OUT]
        S_M2 = [S_M1[0] + SL_M1]
        S_KV = S_M2[0] + SL_M2
        S_Q = S_KV + SL_KV
        S_O = S_Q + SL_Q
        S_M1.append(S_O + SL_O)
        S_M2.append(S_M1[1] + SL_M1)
        B_OUT = SL_IN
        B_M1 = [B_OUT + KC]
        B_M2 = [B_M1[0] + SL_M1]
        B_KV = B_M2[0] + KC
        B_Q = B_KV + SL_KV
        B_O = B_Q + SL_Q
        B_M1.append(B_O + KC)
        B_M2.append(B_M1[1] + SL_M1)

        PARAM_TILES = ((dtw, "dtw"), (dtb, "dtb"), (ident[:, :], "ident"), (triu[:, :, :], "triu"),
                       (low[:, :, :], "low"), (smask, "smask"), (cst, "cst"), (cw, "cw"), (cb, "cb"),
                       (nw, "nw"), (dsk, "dsk"), (lng[:, :, :], "lng"), (lnb[:, :, :], "lnb"))
        N_PARAMS = len(PARAM_TILES)

        ATT_TILES = ((eb, "eb"), (ef, "ef"), (gw, "gw"), (cw1, "cw1"), (cw2, "cw2"), (cpe, "cpe"),
                     (cvalid, "cvalid"), (wmask, "wmask"))

        s_x = sem("x_loaded")
        s_par = sem("params_loaded")
        w_ready = [sem(f"slot_ready{i}") for i in range(NSLOT)]
        w_used = sem("slots_used")
        blk_evac = sem("block_evacuated")
        dve_step = sem("dve_step")
        act_step = sem("act_step")
        s_const = sem("constants_set")
        dt_done = sem("dt_projected")
        dt_abs = sem("dt_exp_ready")
        dt_ready = sem("dt_and_a_ready")
        dt_tr = sem("dt_transposed")
        dt_tok_ready = sem("dt_by_token")
        am_ready = sem("a_by_sequence")
        dec_sum = sem("decay_sums")
        dec_ready = sem("decays_ready")
        conv_done = sem("conv_summed")
        xbc_ready = sem("xbc_ready")
        ah_ready = sem("segment_rows_ready")
        tr_done = sem("x_b_and_cb_summed")
        seg_done = sem("segment_sums")
        ac_done = sem("running_sums")
        btok_ready = sem("b_by_token")
        lm_ready = sem("segment_decays")
        e_ready = sem("running_decays")
        xdt_ready = sem("xdt_ready")
        g_masked = sem("cb_masked")
        m_ready = sem("mix_ready")
        xdec_ready = sem("xdec_ready")
        y_done = sem("y_summed")
        y_read = sem("y_banks_read")
        y_gated = sem("y_gated")
        sst_done = sem("state_summed")
        stmp_ready = sem("state_decayed")
        st_ready = sem("state_ready")
        bm_ready = sem("b_by_sequence")
        sd_loaded = sem("old_states_loaded")
        sd_stored = sem("new_states_stored")
        nsq_ready = sem("y_squared")
        nsq_used = sem("y_squares_summed")
        nvar_ready = sem("y_variance")
        nroot_ready = sem("y_root")
        y_normed = sem("y_normed")
        ln_mean = sem("ln_mean_summed")
        ln_mu = sem("ln_mean_ready")
        ln_cent = sem("ln_centered")
        ln_sq = sem("ln_squared")
        ln_used = sem("ln_squares_summed")
        ln_var = sem("ln_variance")
        ln_root = sem("ln_root")
        ln_scaled = sem("ln_scaled")
        x_ready = sem("stream_ready")
        hid_ready = sem("hidden_ready")
        outs = sem("outputs_stored")

        x_out = sem("result_stored")
        s_tab = sem("attention_params_loaded")
        s_ptab = sem("page_table_loaded")
        negb_set = sem("mask_row_set")
        bt_done = sem("bias_table_summed")
        bt_ready = sem("bias_table_ready")
        bt_stored = sem("bias_table_stored")
        skew_stored = sem("bias_rows_repeated")
        rows_loaded = sem("new_bias_rows_loaded")
        strips_loaded = sem("bias_strips_loaded")
        bd_ready = sem("new_bias_ready")
        cbt_done = sem("compressed_bias_summed")
        cbt_ready = sem("compressed_bias_ready")
        gate_done = sem("gates_summed")
        gate_exp = sem("gates_exp")
        gate_ready = sem("gates_ready")
        gate_stored = sem("gates_stored")
        gn_loaded = sem("new_gates_loaded")
        vt_done = sem("v_transposed")
        vt_ready = sem("v_by_token")
        ct_loaded = [sem(f"compression_rows{i}") for i in range(2)]
        zx_ready = sem("crossing_rows_ready")
        tp_ready = sem("own_half_rows_ready")
        tp_loaded = sem("crossed_rows_loaded")
        pe_done = sem("position_sums")
        hpe_ready = sem("position_bias_ready")
        ch_done = [sem(f"compress_hidden{i}") for i in range(2)]
        ch_sum = [sem(f"compress_hidden_added{i}") for i in range(2)]
        ch_ready = [sem(f"compress_hidden_ready{i}") for i in range(2)]
        cc_done = sem("compressed_summed")
        cc_ready = sem("compressed_ready")
        pcs_done = sem("compressed_scores")
        pc_sub = sem("compressed_scores_shifted")
        pc_exp = sem("compressed_exp")
        pc_ready = sem("compressed_probs")
        sc_done = sem("scores_done")
        sc_read = sem("scores_read")
        mx_ready = sem("maxima_ready")
        ex_done = sem("exp_done")
        wt_ready = sem("weights_ready")
        pn_ready = sem("probs_ready")
        tp_done = [sem(f"probs_transposed{i}") for i in range(2)]
        pt_ready = [sem(f"probs_by_key{i}") for i in range(2)]
        pv_done = sem("probs_used")
        o_ready = sem("o_ready")
        kv_loaded = [sem(f"cache_rows_loaded{i}") for i in range(2)]
        win_stored = [sem(f"window_rows_stored{i}") for i in range(2)]
        nsc_done = sem("new_scores_done")
        nsc_read = sem("new_scores_read")
        nmx_ready = sem("new_maxima_ready")
        nex_done = sem("new_exp_done")
        npn_ready = sem("new_probs_ready")
        ntp_done = sem("new_probs_transposed")
        npt_act = sem("new_probs_by_key_a")
        npt_dve = sem("new_probs_by_key_b")
        no_done = sem("new_o_summed")
        no_ready = sem("new_o_ready")

        block = ctx.enter_context(nc.Block())
        steps = {"dve": 0, "act": 0}

        def link(eng, who, ins):
            s = dve_step if who == "dve" else act_step
            ins.then_inc(s, 1)
            steps[who] += 1
            eng.wait_ge(s, steps[who])

        def width(c):
            return P if c < 4 else ND

        def tok(c):
            return slice(c * P, c * P + width(c))

        def by_seq(v):
            return v.rearrange("p (b i) -> p b i", b=NB)

        def heads(v, d):
            return v.rearrange("p (h d) -> p h d", d=d)

        def over_heads(v, L, n):
            return v.unsqueeze(2).to_broadcast([L, HPG, n])

        def states_before(n):
            g, c = divmod(n, NT)
            return g * (4 + NB) + c

        ITEMS = []
        for qt in range(4):
            for g in range(NKV):
                for br in range(2):
                    ITEMS.append((qt, g, br, len(ITEMS)))

        def prob_tiles(u):
            t0 = sum(qt + 1 + (br == 0) for qt, _, br, _ in ITEMS[:u])
            return t0, t0 + ITEMS[u][0] + 1 + (ITEMS[u][2] == 0)

        COMPRESSED_TILES = {prob_tiles(u)[0] for _, _, br, u in ITEMS if br == 0}

        def tile_rows(t):
            return NCMP if t in COMPRESSED_TILES else P

        def half_of(g):
            return slice((g % 2) * HD, (g % 2) * HD + HD)

        TILES = [(g, c, g * NT + c) for g in range(MG) for c in range(NT)]

        def raw_new(j):
            return raw[j][:, 3 + NP_TOK:].rearrange("p (b i) -> p b i", b=NB)

        @block.sync
        def _(sp):
            for j in range(NSLOT):
                sp.dma_start(ring[:, j, :], a["w"][j, :, :]).then_inc(w_ready[j], 16)

            def stream(first, last):
                with sp.Fori(first // NSLOT, last // NSLOT) as i:
                    for j in range(NSLOT):
                        sp.wait_ge(w_used, i * NSLOT + (j + 1 - NSLOT))
                        sp.dma_start(ring[:, j, :], a["w"][i * NSLOT + j, :, :]).then_inc(w_ready[j], 16)

            stream(NSLOT, S_O + NSLOT)
            sp.wait_ge(s_ptab, 16)
            sp.wait_ge(cc_ready, NB + 1)
            for b in range(NB):
                if b >= 2:
                    sp.wait_ge(no_done, b - 1)
                    sp.wait_ge(win_stored[b % 2], 16 * (b // 2))
                for pg in range(NPG):
                    page = sp.value_load(ptab[0:1, b * NPG + pg:b * NPG + pg + 1], min_val=0, max_val=NPHYS - 1)
                    sp.dma_start(skv[b % 2][:, pg, :], a["sel"][page, :, :]).then_inc(kv_loaded[b % 2], 16)
                sp.dma_start(wkv[b % 2], a["win"][b, :, :, :]).then_inc(kv_loaded[b % 2], 16)
            stream(S_O + NSLOT, N_SLOTS)

        @block.gpsimd
        def _(pool):
            pool.memset(ones[:, :], 1.0)
            pool.memset(onesd[:, :], 1.0 / D)
            pool.memset(raw[0][:, 0:3], 0.0)
            pool.memset(raw[1][:, 0:3], 0.0).then_inc(s_const, 1)

            def load_states(g):
                if g:
                    pool.wait_ge(sd_stored, 16 * g)
                pool.dma_start(sdec, a["state"][:, :, g * 512:(g + 1) * 512]
                               .rearrange("b n m -> n b m")).then_inc(sd_loaded, 16)

            def segment_rows(g, c, n):
                L = width(c)
                if n:
                    pool.wait_ge(ac_done, n)
                pool.tensor_copy(heads(AR[0:L, :], MP), over_heads(a_tok[0:L, c, g * HPG:(g + 1) * HPG], L, MP))
                pool.tensor_tensor(AH[0:L, :, 0:L],
                                   low[0:L, c // 4, 0:L].unsqueeze(1).to_broadcast([L, HPG, L]),
                                   over_heads(a_tok[0:L, c, g * HPG:(g + 1) * HPG], L, L),
                                   ALU.mult).then_inc(ah_ready, 1)

            load_states(0)
            pool.wait_ge(s_par, 16 * N_PARAMS)
            pool.wait_ge(dt_tok_ready, 1)
            pool.tensor_tensor(am, a_tok[0:ND, 4, :].unsqueeze(1).to_broadcast([ND, NB, MH]),
                               smask.unsqueeze(2).to_broadcast([ND, NB, MH]), ALU.mult).then_inc(am_ready, 1)
            pool.wait_ge(dec_ready, 1)
            segment_rows(0, 0, 0)
            for g, c, n in TILES:
                L = width(c)
                pool.wait_ge(xdt_ready, n + 1)
                pool.tensor_tensor(heads(xdec[0:L, :], MP), heads(xdt[0:L, :], MP),
                                   over_heads(dec_tok[0:L, c, g * HPG:(g + 1) * HPG], L, MP),
                                   ALU.mult).then_inc(xdec_ready, 1)
                if c == 4:
                    pool.wait_ge(btok_ready, n + 1)
                    pool.tensor_tensor(Bm, Btok[0:ND, :].unsqueeze(1).to_broadcast([ND, NB, P]),
                                       smask.unsqueeze(2).to_broadcast([ND, NB, P]), ALU.mult
                                       ).then_inc(bm_ready, 1)
                if n + 1 < len(TILES):
                    segment_rows(*TILES[n + 1])
                if 1 <= c < 4:
                    pool.wait_ge(st_ready, states_before(n))
                    pool.tensor_tensor(heads(tmp[0], MP), heads(st[:, g, :], MP),
                                       over_heads(tot[:, c, g * HPG:(g + 1) * HPG], P, MP),
                                       ALU.mult).then_inc(stmp_ready, 1)
                if c == 4:
                    pool.wait_ge(sd_loaded, 16 * (g + 1))
                    for b in range(NB):
                        pool.wait_ge(st_ready, states_before(n) + max(b - 1, 0))
                        pool.tensor_tensor(heads(tmp[b % 2], MP), heads(sdec[:, b, :], MP),
                                           over_heads(totd[:, b, g * HPG:(g + 1) * HPG], P, MP),
                                           ALU.mult).then_inc(stmp_ready, 1)
                    pool.wait_ge(st_ready, states_before(n) + NB)
                    pool.dma_start(a["o_sssm"][:, :, g * 512:(g + 1) * 512].rearrange("b n m -> n b m"),
                                   sdec).then_inc(sd_stored, 16)
                    if g + 1 < MG:
                        load_states(g + 1)
            pool.dma_start(a["o_pssm"], st.rearrange("p g m -> p (g m)")).then_inc(outs, 16)
            pool.wait_ge(conv_done, NXB)
            pool.dma_start(a["o_pconv"], lastp).then_inc(outs, 16)
            pool.dma_start(a["o_sconv"], lastd).then_inc(outs, 16)
            pool.wait_ge(sd_stored, 16 * MG)
            pool.wait_ge(outs, 48)
            pool.wait_ge(blk_evac, B_OUT + KC)
            pool.dma_start(ptab[:, :], a["ptab"]).then_inc(s_ptab, 16)
            pool.memset(relb, NEG).then_inc(negb_set, 1)
            pool.wait_ge(negb_set, 1)
            pool.dma_start(relb[0:NBK, :], a["relb"]).then_inc(s_tab, 16)
            for dst, name in ATT_TILES:
                pool.dma_start(dst, a[name]).then_inc(s_tab, 16)
            pool.wait_ge(s_ptab, 16)

            def load_rows(b):
                for pg in range(NPG):
                    page = pool.value_load(ptab[0:1, b * NPG + pg:b * NPG + pg + 1], min_val=0, max_val=NPHYS - 1)
                    pool.dma_start(ct[b % 2][:, pg, :], a["cmp"][page, :, :]).then_inc(ct_loaded[b % 2], 16)

            pool.memset(h1s[0][:, :, NCMP:NCMP + 1], 0.0)
            pool.memset(h1s[1][:, :, NCMP:NCMP + 1], 0.0).then_inc(s_const, 1)
            pool.memset(bdn, NEG).then_inc(negb_set, 1)
            load_rows(0)
            load_rows(1)
            pool.wait_ge(rows_loaded, 16 * NH)
            pool.wait_ge(s_tab, 16 * (1 + len(ATT_TILES)))
            pool.wait_ge(negb_set, 2)
            pool.tensor_copy(bd[:, 0:PAST - P], nr[:, 0:1].to_broadcast([P, PAST - P]))
            pool.tensor_copy(bd[:, PAST - P:PAST], nr[:, 0:P])
            pool.tensor_copy(bdw[:, NS:PAST - P], nr[:, 0:1].to_broadcast([P, PAST - P - NS]))
            pool.tensor_copy(bdw[:, PAST - P:PAST], nr[:, 0:P])
            pool.tensor_tensor(bdw[:, 0:NS], nr[:, 0:1].to_broadcast([P, NS]), wmask, ALU.add)
            c0 = FARC * CS - (PAST - P - CL + 1)
            pool.tensor_copy(bdc[:, 0:FARC], nr[:, 0:1].to_broadcast([P, FARC]))
            pool.tensor_copy(bdc[:, FARC:NCMP], nr[:, c0:c0 + CS * (NCMP - FARC - 1) + 1:CS])
            pool.tensor_copy(bdn.rearrange("p (b k) -> p b k", k=72)[:, :, 0:NS],
                             nr[:, P:P + NS].unsqueeze(1).to_broadcast([P, NB, NS])).then_inc(bd_ready, 1)
            pool.wait_ge(zx_ready, 8)
            for half in range(2):
                d = (1 - half) * HD
                v = tp[d:d + HD].rearrange("p k g j c -> p (k g) (j c)") \
                    .rearrange("p (m h) x -> p m h x", h=2)[:, :, half, :]
                pool.dma_start(v, zx[half * HD:half * HD + HD, :, :]).then_inc(tp_loaded, 16)
            pool.wait_ge(blk_evac, B_Q)
            pool.dma_start(a["o_kv"], kvT).then_inc(outs, 16)
            for b in range(2, NB):
                pool.wait_ge(ch_done[1], b - 1)
                load_rows(b)
            pool.wait_ge(gate_ready, 1)
            pool.dma_start(a["gscr"], gates[0:ND, 4, :]).then_inc(gate_stored, 16)
            pool.wait_ge(gate_stored, 16)
            for h in range(NH):
                src = bass.AP(a["gscr"].tensor, 3 * h, [[3 * NH, NS], [NS * 3 * NH, NB], [1, 3]])
                pool.dma_start(gn[h * NS:(h + 1) * NS, :, :], src).then_inc(gn_loaded, 16)
            for qt, g, br, u in ITEMS:
                n = (qt + 1) * P
                pool.wait_ge(wt_ready, u + 1)
                pool.tensor_tensor(Pb[u % 2][:, :, 0:n], Pb[u % 2][:, :, 0:n],
                                   wt[:, u % 2, :].unsqueeze(2).to_broadcast([P, GR, n]), ALU.mult
                                   ).then_inc(pn_ready, 1)
            for b in range(NB):
                pool.wait_ge(kv_loaded[b % 2], 80 * (b // 2 + 1))
                pool.dma_start(a["o_win"][b, :, :, :], wkv[b % 2]).then_inc(win_stored[b % 2], 16)
            pool.wait_ge(win_stored[0], 16 * NB // 2)
            pool.wait_ge(win_stored[1], 16 * NB // 2)
            pool.wait_ge(outs, 64)
            pool.wait_ge(x_ready, 4 * KC)
            pool.dma_start(a["o_y"], xT[:, :, :]).then_inc(x_out, 16)
            pool.wait_ge(x_out, 16)

        @block.scalar
        def _(act):
            act.dma_start(xT[:, :, :], a["x"]).then_inc(s_x, 16)
            for dst, name in PARAM_TILES:
                act.dma_start(dst, a[name]).then_inc(s_par, 16)

            act.wait_ge(s_par, 16 * N_PARAMS)
            act.wait_ge(dt_done, 1)
            act.activation(dtT[:, 0:NP_TOK], bD[1][0:MH, :], ACT.Identity, bias=dtb[:, 0:1])
            link(act, "act", act.activation(dtT[:, NP_TOK:T], bDn[0:MH, 1, 0:ND], ACT.Identity, bias=dtb[:, 0:1]))
            link(act, "act", act.activation(dw[0], dtT, ACT.Abs))
            act.activation(dw[1], dw[0], ACT.Exp, scale=-1.0)
            act.activation(dtb[:, 1:2], dtb[:, 1:2], ACT.Exp).then_inc(dt_abs, 1)

            def evac(blk):
                g, j = divmod(blk, GB)
                par = blk % 2
                act.wait_ge(w_used, blk + 1)
                if j < XB:
                    x = g * XB + j
                    if x >= 2:
                        act.wait_ge(conv_done, x - 1)
                    act.activation(raw_new(x % 2)[:, :, 0:3], cst[:, x, :, :], ACT.Copy)
                    act.activation(raw[x % 2][:, 3:3 + NP_TOK], bD[par][:, :], ACT.Copy)
                    act.activation(raw_new(x % 2)[:, :, 3:3 + NS], by_seq(bDn[:, par, 0:ND]), ACT.Copy
                                   ).then_inc(blk_evac, 1)
                else:
                    m = g * 4 + j - XB
                    act.activation(y[:, m, 0:NP_TOK], bD[par][:, :], ACT.Silu)
                    act.activation(y[:, m, NP_TOK:T], bDn[:, par, 0:ND], ACT.Silu).then_inc(blk_evac, 1)

            def conv_silu(blk):
                g, j = divmod(blk, GB)
                if j >= XB:
                    return
                x = g * XB + j
                act.wait_ge(conv_done, x + 1)
                if g >= 2:
                    act.wait_ge(y_gated, (g - 1) * NT)
                act.activation(xbc[g % 2][:, j, :], acc[x % 2], ACT.Silu).then_inc(xbc_ready, 1)

            act.wait_ge(dec_sum, 1)
            act.activation(dec_tok[:, 0:4, :].rearrange("p c h -> p (c h)"), bS[:, 0, 0:4 * MH], ACT.Exp)
            act.activation(dec_tok[0:ND, 4, :], bS[0:ND, 0, 4 * MH:NT * MH], ACT.Exp)
            act.activation(tot.rearrange("p c h -> p (c h)"), bS[:, 0, NT * MH:(NT + 4) * MH], ACT.Exp)
            act.activation(totd.rearrange("p b h -> p (b h)"), bS[:, 1, 0:NB * MH], ACT.Exp
                           ).then_inc(dec_ready, 1)
            for blk in range(GB):
                evac(blk)
                if blk:
                    conv_silu(blk - 1)
            for g, c, n in TILES:
                L = width(c)
                for half in range(2):
                    act.wait_ge(seg_done, 2 * n + half + 1)
                    act.activation(Lm[0:L, half * 4:half * 4 + 4, 0:L],
                                   bS[0:L, half, 0:4 * L].rearrange("p (h l) -> p h l", h=4),
                                   ACT.Exp).then_inc(lm_ready, 1)
                act.wait_ge(ac_done, n + 1)
                act.activation(E[:, 0:4 * L], bX[:, 0:4 * L], ACT.Exp).then_inc(e_ready, 1)
                if g + 1 < MG:
                    for blk in ((g + 1) * GB + 2 * c, (g + 1) * GB + 2 * c + 1):
                        evac(blk)
                        conv_silu(blk - 1)
                if c == 4:
                    act.wait_ge(y_gated, n + 1)
                    for m in range(4):
                        if g * 4 + m >= 2:
                            act.wait_ge(nsq_used, g * 4 + m - 1)
                        act.activation(sq[:, m % 2, :], y[:, g * 4 + m, :], ACT.Square).then_inc(nsq_ready, 1)
                    act.wait_ge(nvar_ready, g + 1)
                    act.activation(row[:, :], row[:, :], ACT.Sqrt).then_inc(nroot_ready, 1)

            def layer_norm(k):
                act.wait_ge(ln_mean, k + 1)
                act.activation(row[:, 0:NP_TOK], bS[:, 0, :], ACT.Copy)
                act.activation(row[:, NP_TOK:T], bM[:, 0:ND], ACT.Copy).then_inc(ln_mu, 1)
                for m in range(KC):
                    act.wait_ge(ln_cent, k * KC + m + 1)
                    if m >= 2:
                        act.wait_ge(ln_used, k * KC + m - 1)
                    act.activation(sq[:, m % 2, :], xT[:, m, :], ACT.Square).then_inc(ln_sq, 1)
                act.wait_ge(ln_var, k + 1)
                act.activation(row[:, :], row[:, :], ACT.Sqrt).then_inc(ln_root, 1)
                for m in range(KC):
                    act.wait_ge(ln_scaled, k * KC + m + 1)
                    act.activation(xT[:, m, :], xT[:, m, :], ACT.Identity, bias=lnb[:, k, m:m + 1],
                                   scale=lng[:, k, m:m + 1]).then_inc(x_ready, 1)

            layer_norm(0)
            act.wait_ge(bt_ready, 1)
            act.dma_start(a["bscr"], bt).then_inc(bt_stored, 16)
            act.wait_ge(bt_stored, 16)
            y0 = Y0 - 2 * P + 1
            act.dma_start(a["bskew"], bass.AP(a["bscr"].tensor, y0, [[0, P], [XN, NH], [1, RW]])
                          ).then_inc(skew_stored, 16)
            act.wait_ge(skew_stored, 16)
            act.dma_start(Rs, bass.AP(a["bskew"].tensor, P - 1, [[NH * RW - 1, P], [RW, NH], [1, RB]])
                          ).then_inc(strips_loaded, 16)
            act.wait_ge(strips_loaded, 16)
            for h in range(NH):
                act.dma_start(nr[h * NS:(h + 1) * NS, :], Rs[0:NS, h, 0:P + 2 * NS]).then_inc(rows_loaded, 16)
            layer_norm(1)

            act.wait_ge(blk_evac, B_Q)
            for own in range(2):
                for m in range(4):
                    kv, gp = divmod(m, 2)
                    for half in range(2):
                        ps = slice(half * HD, half * HD + HD)
                        src = kvT[ps, m, 0:NP_TOK].rearrange("p (c j h) -> p j h c", c=NCMP, h=2)
                        if own:
                            act.activation(tp[ps, kv, 2 * gp + half, :, :], src[:, :, half, :], ACT.Copy
                                           ).then_inc(tp_ready, 1)
                        else:
                            act.activation(zx[ps, m, :].rearrange("p (j c) -> p j c", j=8),
                                           src[:, :, 1 - half, :], ACT.Copy).then_inc(zx_ready, 1)

            act.wait_ge(gate_done, 1)
            act.activation(gates[:, 0:4, :].rearrange("p c h -> p (c h)"), bM[:, 0:4 * 3 * NH], ACT.Exp, scale=-1.0)
            act.activation(gates[0:ND, 4, :], bM[0:ND, 4 * 3 * NH:5 * 3 * NH], ACT.Exp, scale=-1.0
                           ).then_inc(gate_exp, 1)

            for s_ in range(NB + 1):
                for kv in range(2):
                    act.wait_ge(ch_sum[kv], s_ + 1)
                    act.activation(hs[kv].rearrange("p g c -> p (g c)"), hs[kv].rearrange("p g c -> p (g c)"),
                                   ACT.Silu, bias=hpe[:, kv:kv + 1]).then_inc(ch_ready[kv], 1)

            def copy_probs(t):
                if t % 2 == 0:
                    act.wait_ge(tp_done[0], t // 2 + 1)
                    if t >= 4:
                        act.wait_ge(pv_done, t - 3)
                    n = tile_rows(t)
                    act.activation(PT[t % 4][0:n, :], bX[0:n, :], ACT.Copy).then_inc(pt_ready[0], 1)

            def exps(u):
                qt, g, br, _ = ITEMS[u]
                n = (qt + 1) * P
                act.wait_ge(mx_ready, u + 1)
                for r in range(GR):
                    last = act.activation(Pb[u % 2][:, r, 0:n], Pb[u % 2][:, r, 0:n], ACT.Exp,
                                          bias=nmx[:, u % 2, r:r + 1], accum_out=sm[:, u % 2, r:r + 1])
                last.then_inc(ex_done, 1)

            exps(0)
            for u in range(len(ITEMS)):
                qt, g, br, _ = ITEMS[u]
                if u % 8 == 0:
                    act.wait_ge(pc_sub, qt + 1)
                    act.activation(Pc.rearrange("p h c -> p (h c)"), Pc.rearrange("p h c -> p (h c)"), ACT.Exp
                                   ).then_inc(pc_exp, 1)
                if u + 1 < len(ITEMS):
                    exps(u + 1)
                for t in range(prob_tiles(u)[0], prob_tiles(u)[1]):
                    copy_probs(t)
                if u % 4 == 3:
                    act.wait_ge(pv_done, prob_tiles(u)[1])
                    gp = g // 2
                    act.activation(qT[:, gp * GR:(gp + 1) * GR, tok(qt)],
                                   bDn[:, (u // 4) % 2, :].rearrange("p (r q) -> p r q", r=GR), ACT.Copy
                                   ).then_inc(o_ready, 1)

            def new_exps(b):
                act.wait_ge(nmx_ready, b + 1)
                p_ = Pd[b % 2]
                W = PAST + ND
                for i, (lo, hi) in enumerate(((0, W), (W, 2 * W), (2 * W, 2 * W + NCMP))):
                    last = act.activation(p_[:, lo:hi], p_[:, lo:hi], ACT.Exp, bias=dnm[:, i:i + 1],
                                          accum_out=dsm[:, i:i + 1])
                last.then_inc(nex_done, 1)

            new_exps(0)
            for b in range(NB):
                act.wait_ge(ntp_done, b + 1)
                act.activation(PTd[:, 0:PAST], bX[:, :], ACT.Copy)
                act.activation(PTs[0:ND, 0:2 * P], bDn[0:ND, 1, 0:2 * P], ACT.Copy)
                act.activation(PTs[0:NCMP, 2 * P:3 * P], bDn[0:NCMP, 1, 2 * P:3 * P], ACT.Copy
                               ).then_inc(npt_act, 1)
                if b + 1 < NB:
                    new_exps(b + 1)
                act.wait_ge(no_done, b + 1)
                act.activation(qT[:, :, NP_TOK + b * NS:NP_TOK + (b + 1) * NS],
                               bDn[:, 0, 0:2 * GR * NS].rearrange("p (m i) -> p m i", i=NS), ACT.Copy
                               ).then_inc(no_ready, 1)
            layer_norm(2)
            layer_norm(3)

        @block.tensor
        def _(pe):
            def dense_block(blk, par, rnd, j0, nsl, rhs):
                if not (isinstance(blk, int) and blk < 2):
                    pe.wait_ge(blk_evac, blk - 1)
                for s in range(nsl):
                    j = (j0 + s) % NSLOT
                    pe.wait_ge(w_ready[j], rnd * 16 + (16 * ((j0 + s) // NSLOT) + 16))
                    for k in range(KC):
                        kk = s * KC + k
                        w = ring[:, j, k * P:(k + 1) * P]
                        ends = dict(start=kk == 0, stop=kk == nsl * KC - 1)
                        pe.matmul(bD[par][:, :], w, rhs[:, kk, 0:NP_TOK], **ends)
                        mm = pe.matmul(bDn[:, par, 0:ND], w, rhs[:, kk, NP_TOK:T], **ends)
                    mm.then_inc(w_used, 1)

            def in_block(blk):
                dense_block(blk, blk % 2, blk // NSLOT, blk % NSLOT, 1, xT)

            pe.wait_ge(s_x, 16)
            pe.wait_ge(s_par, 16 * N_PARAMS)
            for k in range(KC):
                ends = dict(start=k == 0, stop=k == KC - 1)
                pe.matmul(bD[1][0:MH, :], dtw[:, k, :], xT[:, k, 0:NP_TOK], **ends)
                mm = pe.matmul(bDn[0:MH, 1, 0:ND], dtw[:, k, :], xT[:, k, NP_TOK:T], **ends)
            mm.then_inc(dt_done, 1)
            in_block(0)
            pe.wait_ge(dt_ready, 1)
            for c in range(NT):
                L = width(c)
                pe.transpose(bX[0:L, c * 64:c * 64 + MH], dtT[:, tok(c)], ident[0:MH, 0:MH])
                mm = pe.transpose(bX[0:L, c * 64 + MH:c * 64 + 64], aT[:, tok(c)], ident[0:MH, 0:MH])
            mm.then_inc(dt_tr, 1)
            in_block(1)
            pe.wait_ge(am_ready, 1)
            pe.wait_ge(s_const, 1)
            for c in range(NT):
                L = width(c)
                pe.matmul(bS[0:L, 0, c * MH:(c + 1) * MH], low[0:L, c // 4, 0:L], a_tok[0:L, c, :],
                          start=True, stop=True)
            for c in range(4):
                pe.matmul(bS[:, 0, (NT + c) * MH:(NT + c + 1) * MH], ones[:, :], a_tok[:, c, :],
                          start=True, stop=True)
            pe.matmul(bS[:, 1, 0:NB * MH], ones[0:ND, :], am.rearrange("p b h -> p (b h)"),
                      start=True, stop=True).then_inc(dec_sum, 1)
            for blk in range(2, GB):
                in_block(blk)

            def inner_sums(g, c, n):
                L = width(c)
                xg = xbc[g % 2]
                if c == 0:
                    pe.wait_ge(xbc_ready, (g + 1) * XB)
                if n:
                    pe.wait_ge(y_read, n)
                    pe.wait_ge(st_ready, states_before(n - 1) + (NB if (n - 1) % NT == 4 else 1))
                else:
                    pe.wait_ge(dec_ready, 1)
                if c == 0 and g:
                    pe.wait_ge(nvar_ready, g)
                for j in range(4):
                    pe.transpose(bX[0:L, j * P:(j + 1) * P], xg[:, j, tok(c)], ident[:, :])
                pe.transpose(bM[0:L, 0:P], xg[:, 4, tok(c)], ident[:, :])
                pe.matmul(bM[0:L, P:P + L], xg[:, 4, tok(c)], xg[:, 5, tok(c)], start=True, stop=True
                          ).then_inc(tr_done, 1)
                pe.wait_ge(ah_ready, n + 1)
                for h in range(HPG):
                    mm = pe.matmul(bS[0:L, h // 4, (h % 4) * L:(h % 4 + 1) * L], AH[0:L, h, 0:L],
                                   triu[0:L, c // 4, 0:L], start=True, stop=True)
                    if h % 4 == 3:
                        mm.then_inc(seg_done, 1)
                pe.wait_ge(xdt_ready, n + 1)
                for j in range(4):
                    mm = pe.matmul(bX[:, j * L:(j + 1) * L],
                                   AR[0:L, j * P:(j + 1) * P],
                                   triu[0:L, c // 4, 0:L], start=True, stop=True)
                mm.then_inc(ac_done, 1)

            def outer_sums(g, c, n):
                L = width(c)
                xg = xbc[g % 2]
                pe.wait_ge(m_ready, n + 1)
                for h in range(HPG):
                    p0 = (h % 2) * MP
                    mm = pe.matmul(bS[p0:p0 + MP, 0, (h // 2) * L:(h // 2 + 1) * L],
                                   xdt[0:L, h * MP:(h + 1) * MP], Lm[0:L, h, 0:L], start=True, stop=True)
                if 1 <= c < 4:
                    pe.wait_ge(st_ready, states_before(n))
                    for j in range(4):
                        mm = pe.matmul(bS[:, 1, j * L:(j + 1) * L], st[:, g, j * P:(j + 1) * P],
                                       xg[:, 5, tok(c)], start=True, stop=True)
                if c == 4:
                    pe.wait_ge(sd_loaded, 16 * (g + 1))
                    for b in range(NB):
                        for j in range(4):
                            mm = pe.matmul(bS[:, 1, j * L + b * NS:j * L + (b + 1) * NS],
                                           sdec[:, b, j * P:(j + 1) * P],
                                           xg[:, 5, NP_TOK + b * NS:NP_TOK + (b + 1) * NS],
                                           start=True, stop=True)
                mm.then_inc(y_done, 1)
                pe.wait_ge(xdec_ready, n + 1)
                pe.wait_ge(e_ready, n + 1)
                if c < 4:
                    pe.wait_ge(btok_ready, n + 1)
                    pe.matmul(bX[:, :], Btok[0:L, :], xdec[0:L, :], start=True, stop=True).then_inc(sst_done, 1)
                else:
                    pe.wait_ge(bm_ready, g + 1)
                    for b in range(NB):
                        if b >= 2:
                            pe.wait_ge(st_ready, states_before(n) + b - 1)
                        pe.matmul((bX, bM)[b % 2][:, :], Bm[:, b, :], xdec[0:L, :], start=True, stop=True
                                  ).then_inc(sst_done, 1)

            for g, c, n in TILES:
                inner_sums(g, c, n)
                if g + 1 < MG:
                    in_block((g + 1) * GB + 2 * c)
                outer_sums(g, c, n)
                if g + 1 < MG:
                    in_block((g + 1) * GB + 2 * c + 1)
                if c == 4:
                    pe.wait_ge(y_gated, n + 1)
                    pe.wait_ge(st_ready, states_before(n) + NB)
                    for m in range(4):
                        pe.wait_ge(nsq_ready, g * 4 + m + 1)
                        pe.matmul(bS[:, 0, :], ones[:, :], sq[:, m % 2, 0:NP_TOK], start=m == 0, stop=m == 3)
                        pe.matmul(bM[:, 0:ND], ones[:, :], sq[:, m % 2, NP_TOK:T], start=m == 0, stop=m == 3
                                  ).then_inc(nsq_used, 1)

            pe.wait_ge(y_normed, MG)
            with pe.Fori(0, KC // 2) as i:
                for j in range(2):
                    dense_block(i * 2 + (B_OUT + j), j, i + S_OUT // NSLOT, 2 * j, 2, y)

            def layer_norm(k, blocks):
                if k == 1:
                    pe.wait_ge(cbt_ready, 1)
                pe.wait_ge(blk_evac, blocks)
                for m in range(KC):
                    pe.matmul(bS[:, 0, :], onesd[:, :], xT[:, m, 0:NP_TOK], start=m == 0, stop=m == KC - 1)
                    mm = pe.matmul(bM[:, 0:ND], onesd[:, :], xT[:, m, NP_TOK:T], start=m == 0, stop=m == KC - 1)
                mm.then_inc(ln_mean, 1)
                pe.wait_ge(ln_mu, k + 1)
                for m in range(KC):
                    pe.wait_ge(ln_sq, k * KC + m + 1)
                    pe.matmul(bS[:, 0, :], onesd[:, :], sq[:, m % 2, 0:NP_TOK], start=m == 0, stop=m == KC - 1)
                    pe.matmul(bM[:, 0:ND], onesd[:, :], sq[:, m % 2, NP_TOK:T], start=m == 0, stop=m == KC - 1
                              ).then_inc(ln_used, 1)

            def bias_tables():
                pe.wait_ge(s_tab, 16 * (1 + len(ATT_TILES)))
                pe.wait_ge(ln_var, 1)
                for i, (bank, lo) in enumerate(((bS[:, 0, :], 0), (bS[:, 1, :], 512), (bX[:, :], 1024))):
                    n = min(512, XN - lo)
                    pe.matmul(bank[0:NH, 0:n], relb[:, :], eb[:, lo:lo + n], start=True, stop=True
                              ).then_inc(bt_done, 1)
                pe.wait_ge(bt_ready, 1)
                for i in range(NSIG):
                    o_ = i * NH
                    x0 = X0 + CB0 - CS * i
                    mm = pe.matmul(bS[:, o_ // 512, o_ % 512:o_ % 512 + NH], ef[:, x0:x0 + P], relb[:, :],
                                   start=True, stop=True)
                mm.then_inc(cbt_done, 1)

            def mlp(k):
                pe.wait_ge(x_ready, (2 * k + 1) * KC)
                with pe.Fori(0, SL_M1 // NSLOT) as i:
                    for j in range(NSLOT):
                        dense_block(i * NSLOT + (B_M1[k] + j), j % 2, i + S_M1[k] // NSLOT, j, 1, xT)
                if k == 0:
                    bias_tables()
                pe.wait_ge(hid_ready, (k + 1) * SL_M1)
                with pe.Fori(0, KC // 2) as i:
                    for j in range(2):
                        dense_block(i * 2 + (B_M2[k] + j), j, i * 2 + (S_M2[k] // NSLOT + j), 0, NSLOT, hid)

            layer_norm(0, B_OUT + KC)
            mlp(0)
            layer_norm(1, B_M2[0] + KC)

            pe.wait_ge(x_ready, 2 * KC)
            with pe.Fori(0, SL_KV // NSLOT) as i:
                for j in range(NSLOT):
                    dense_block(i * NSLOT + (B_KV + j), j % 2, i + S_KV // NSLOT, j, 1, xT)
            with pe.Fori(0, SL_Q // NSLOT) as i:
                for j in range(NSLOT):
                    dense_block(i * NSLOT + (B_Q + j), j % 2, i + S_Q // NSLOT, j, 1, xT)
            for c in range(NT):
                for k in range(KC):
                    mm = pe.matmul(bM[0:width(c), c * 48:(c + 1) * 48], xT[:, k, tok(c)], gw[:, k, :],
                                   start=k == 0, stop=k == KC - 1)
            mm.then_inc(gate_done, 1)
            pe.wait_ge(blk_evac, B_Q)
            for c in range(NT):
                if c >= 2:
                    pe.wait_ge(vt_ready, c - 1)
                for j, m in enumerate((6, 7, 10, 11)):
                    mm = pe.transpose(bS[0:width(c), c % 2, j * P:(j + 1) * P], kvT[:, m, tok(c)], ident[:, :])
                mm.then_inc(vt_done, 1)

            pe.wait_ge(s_const, 2)
            for kv in range(2):
                for i in range(16):
                    mm = pe.matmul(bX[:, kv:kv + 1], cw1[:, kv, i // 8, i % 8, :], cpe[:, kv, i // 8, i % 8:i % 8 + 1],
                                   start=i == 0, stop=i == 15)
            mm.then_inc(pe_done, 1)
            pe.wait_ge(vt_ready, NT)

            def hidden(s_):
                if s_ < NB:
                    pe.wait_ge(ct_loaded[s_ % 2], 16 * NPG * (s_ // 2 + 1))
                else:
                    pe.wait_ge(tp_loaded, 32)
                    pe.wait_ge(tp_ready, 8)
                for kv in range(2):
                    if s_:
                        pe.wait_ge(ch_sum[kv], s_)
                    for r in range(2):
                        for j in range(8):
                            if s_ < NB:
                                rows = ct[s_ % 2].rearrange("p g (k j x) -> p g k j x", k=2, j=8)[:, :, kv, j, :]
                            else:
                                rows = tp[:, kv, :, j, :]
                            mm = pe.matmul(bS[:, kv, r * P:(r + 1) * P], cw1[:, kv, r, j, :], rows,
                                           start=j == 0, stop=j == 7)
                    mm.then_inc(ch_done[kv], 1)

            def compressed(s_):
                pe.wait_ge(hpe_ready, 1)
                if s_:
                    pe.wait_ge(cc_ready, s_)
                else:
                    pe.wait_ge(gate_ready, 1)
                pe.wait_ge(ch_ready[0], s_ + 1)
                for half in range(2):
                    pe.matmul(bX[half * HD:half * HD + HD, 0:2 * NCMP], cw2[:, 0, :], hs[0][:, half::2, :],
                              start=True, stop=True)
                pe.wait_ge(ch_ready[1], s_ + 1)
                for g in range(NKV):
                    mm = pe.matmul(bM[0:NCMP, g * HD:(g + 1) * HD], hs[1][:, g, :], cw2[:, 1, :],
                                   start=True, stop=True)
                mm.then_inc(cc_done, 1)

            hidden(0)
            for s_ in range(NB + 1):
                if s_ < NB:
                    hidden(s_ + 1)
                compressed(s_)

            def scores(u):
                qt, g, br, _ = ITEMS[u]
                h_ = half_of(g)
                for r in range(GR):
                    if u:
                        pe.wait_ge(sc_read, 4 * (u - 1) + r + 1)
                    pe.matmul(SB[r][:, 0:(qt + 1) * P], qT[h_, (g // 2) * GR + r, tok(qt)],
                              kvT[h_, 4 * (br + 1) + g // 2, 0:(qt + 1) * P], start=True, stop=True
                              ).then_inc(sc_done, 1)

            def compressed_scores(qt):
                if qt:
                    pe.wait_ge(pt_ready[0], (prob_tiles(8 * qt - 1)[1] + 1) // 2)
                    pe.wait_ge(pt_ready[1], prob_tiles(8 * qt - 1)[1] // 2)
                for h in range(NH):
                    g, r = divmod(h, GR)
                    c0 = ((g // 2) * GR + r) * NCMP
                    mm = pe.matmul((bX, bM)[g % 2][:, c0:c0 + NCMP], qT[half_of(g), (g // 2) * GR + r, tok(qt)],
                                   kc[half_of(g), NB, g // 2, :], start=True, stop=True)
                mm.then_inc(pcs_done, 1)

            pe.wait_ge(cc_ready, NB + 1)
            pe.wait_ge(blk_evac, B_O)
            compressed_scores(0)
            scores(0)
            for u, (qt, g, br, _) in enumerate(ITEMS):
                if u % 8 == 0 and qt:
                    compressed_scores(qt)
                if u + 1 < len(ITEMS):
                    scores(u + 1)
                o_bank = bDn[half_of(g), (u // 4) % 2, :]
                if u % 4 == 0 and u >= 8:
                    pe.wait_ge(o_ready, u // 4 - 1)
                t0, t1 = prob_tiles(u)
                if br == 0:
                    pe.wait_ge(pc_ready, qt + 1)
                if u % 8 == 0:
                    pe.wait_ge(pc_sub, qt + 1)

                def transposes(t):
                    bank = (bX, bM)[t % 2]
                    if t >= 2:
                        pe.wait_ge(pt_ready[t % 2], t // 2)
                    for r in range(GR):
                        if br == 0 and t == t0:
                            mm = pe.transpose(bank[0:NCMP, r * P:(r + 1) * P], Pc[:, g * GR + r, :], ident[:, :])
                        else:
                            kt = t - t0 - (br == 0)
                            mm = pe.transpose(bank[:, r * P:(r + 1) * P], Pb[u % 2][:, r, kt * P:(kt + 1) * P],
                                              ident[:, :])
                    mm.then_inc(tp_done[t % 2], 1)

                def values(t):
                    pe.wait_ge(pt_ready[t % 2], t // 2 + 1)
                    if br == 0 and t == t0:
                        pe.matmul(o_bank, vc[:, NB, g, :], PT[t % 4][0:NCMP, :], start=True, stop=False
                                  ).then_inc(pv_done, 1)
                    else:
                        kt = t - t0 - (br == 0)
                        mm = pe.matmul(o_bank, Vt[:, kt, br, g, :], PT[t % 4][:, :], start=False,
                                       stop=br == 1 and kt == qt)
                        mm.then_inc(pv_done, 1)

                for t in range(t0, t1):
                    if t == t0 + (br == 0):
                        pe.wait_ge(pn_ready, u + 1)
                    transposes(t)
                    if t > t0:
                        values(t - 1)
                values(t1 - 1)
            def new_scores(b):
                pe.wait_ge(kv_loaded[b % 2], 80 * (b // 2 + 1))
                if b:
                    pe.wait_ge(nsc_read, b)
                for g in range(NKV):
                    h_, rows, gp = half_of(g), slice(32 * g, 32 * g + 32), g // 2
                    q = qn[h_, gp, b, :]
                    ks = slice(gp * P, (gp + 1) * P)
                    pe.matmul(bD[0][rows, :], q, skv[b % 2][h_, :, ks], start=True, stop=True)
                    pe.matmul(bD[1][rows, :], q, wkv[b % 2][h_, :, ks], start=True, stop=True)
                    for br in range(2):
                        pe.matmul(bS[rows, 0, br * ND:(br + 1) * ND], q, kvT[h_, 4 * (br + 1) + gp, NP_TOK:T],
                                  start=True, stop=True)
                    mm = pe.matmul(bS[rows, 0, 2 * ND:2 * ND + NCMP], q, kc[h_, b, gp, :], start=True, stop=True)
                mm.then_inc(nsc_done, 1)

            pe.wait_ge(sc_read, GR * len(ITEMS))
            pe.wait_ge(o_ready, len(ITEMS) // 4)
            W = PAST + ND
            new_scores(0)
            for b in range(NB):
                if b + 1 < NB:
                    new_scores(b + 1)
                p_ = Pd[b % 2]
                pe.wait_ge(npn_ready, b + 1)
                for pg in range(NPG):
                    cols = slice(pg * P, (pg + 1) * P)
                    pe.transpose(bX[:, cols], p_[:, cols], ident[:, :])
                    pe.transpose(bM[:, cols], p_[:, W + pg * P:W + (pg + 1) * P], ident[:, :])
                for br in range(2):
                    pe.transpose(bDn[0:ND, 1, br * P:(br + 1) * P], p_[:, br * W + PAST:(br + 1) * W], ident[:, :])
                pe.transpose(bDn[0:NCMP, 1, 2 * P:3 * P], p_[:, 2 * W:2 * W + NCMP], ident[:, :]).then_inc(ntp_done, 1)
                pe.wait_ge(npt_act, b + 1)
                pe.wait_ge(npt_dve, b + 1)
                if b:
                    pe.wait_ge(no_ready, b)
                for g in range(NKV):
                    o_ = bDn[half_of(g), 0, (g // 2) * 32:(g // 2) * 32 + 32]
                    rows = slice(32 * g, 32 * g + 32)
                    vs = slice(256 + g * HD, 256 + (g + 1) * HD)
                    for pg in range(NPG):
                        k0 = pg * P + 32 * g
                        pe.matmul(o_, skv[b % 2][:, pg, vs], PTd[:, k0:k0 + 32], start=pg == 0, stop=False)
                        pe.matmul(o_, wkv[b % 2][:, pg, vs], PTd[:, PAST + k0:PAST + k0 + 32], start=False, stop=False)
                    for br in range(2):
                        pe.matmul(o_, Vt[0:ND, 4, br, g, :], PTs[0:ND, br * P + 32 * g:br * P + 32 * g + 32],
                                  start=False, stop=False)
                    mm = pe.matmul(o_, vc[:, b, g, :], PTs[0:NCMP, 2 * P + 32 * g:2 * P + 32 * g + 32],
                                   start=False, stop=True)
                mm.then_inc(no_done, 1)

            pe.wait_ge(no_ready, NB)
            with pe.Fori(0, SL_O // NSLOT) as i:
                for j in range(NSLOT):
                    dense_block(i * NSLOT + (B_O + j), j % 2, i + S_O // NSLOT, j, 1, qT)
            layer_norm(2, B_O + KC)
            mlp(1)
            layer_norm(3, B_M2[1] + KC)

        @block.vector
        def _(dve):
            dve.wait_ge(dt_abs, 1)
            link(dve, "dve", dve.tensor_scalar(dw[2], dw[1], 2.0, None, ALU.add))
            link(dve, "dve", dve.reciprocal(dw[0], dw[2]))
            link(dve, "dve", dve.tensor_tensor(dw[0], dw[0], dw[1], ALU.mult))
            link(dve, "dve", dve.tensor_tensor(dw[1], dw[0], dw[0], ALU.mult))
            link(dve, "dve", dve.tensor_scalar(dw[2], dw[1], 1.0 / 17, None, ALU.mult))
            for power in (15, 13, 11, 9, 7, 5, 3):
                link(dve, "dve", dve.scalar_tensor_tensor(dw[2], dw[2], 1.0 / power, dw[1], ALU.add, ALU.mult))
            link(dve, "dve", dve.scalar_tensor_tensor(dw[2], dw[2], 1.0, dw[0], ALU.add, ALU.mult))
            dve.tensor_scalar(dw[2], dw[2], 2.0, None, ALU.mult)
            link(dve, "dve", dve.tensor_scalar(dw[3], dtT, 0.0, None, ALU.max))
            link(dve, "dve", dve.tensor_tensor(dtT, dw[2], dw[3], ALU.add))
            dve.tensor_scalar(aT, dtT, dtb[:, 1:2], -1.0, ALU.mult, ALU.mult).then_inc(dt_ready, 1)
            dve.wait_ge(dt_tr, 1)
            tr = bX[:, 0:NT * 64].rearrange("p (c k h) -> p c k h", c=NT, k=2)
            dve.tensor_copy(dt_tok[:, 0:4, :], tr[:, 0:4, 0, :])
            dve.tensor_copy(dt_tok[0:ND, 4, :], tr[0:ND, 4, 0, :])
            dve.tensor_copy(a_tok[:, 0:4, :], tr[:, 0:4, 1, :])
            dve.tensor_copy(a_tok[0:ND, 4, :], tr[0:ND, 4, 1, :]).then_inc(dt_tok_ready, 1)

            def conv(blk):
                g, j = divmod(blk, GB)
                if j >= XB:
                    return
                x = g * XB + j
                r, rn, o = raw[x % 2], raw_new(x % 2), acc[x % 2]
                on = by_seq(o[:, NP_TOK:T])
                dve.wait_ge(blk_evac, blk + 1)
                if x >= 2:
                    dve.wait_ge(xbc_ready, x - 1)
                dve.tensor_copy(lastp[:, x, :], r[:, NP_TOK:NP_TOK + 3])
                dve.tensor_copy(lastd[:, x, :, :], rn[:, :, NS:NS + 3])
                dve.tensor_scalar(o[:, 0:NP_TOK], r[:, 0:NP_TOK], cw[:, x, 0:1], cb[:, x:x + 1],
                                  ALU.mult, ALU.add)
                last = dve.tensor_scalar(on, rn[:, :, 0:NS], cw[:, x, 0:1], cb[:, x:x + 1], ALU.mult, ALU.add)
                for k in range(1, CONV):
                    link(dve, "dve", last)
                    dve.scalar_tensor_tensor(o[:, 0:NP_TOK], r[:, k:k + NP_TOK], cw[:, x, k:k + 1],
                                             o[:, 0:NP_TOK], ALU.mult, ALU.add)
                    last = dve.scalar_tensor_tensor(on, rn[:, :, k:k + NS], cw[:, x, k:k + 1], on,
                                                    ALU.mult, ALU.add)
                last.then_inc(conv_done, 1)

            for blk in range(GB):
                conv(blk)
            for g, c, n in TILES:
                L = width(c)
                xg = xbc[g % 2]
                gh = slice(g * HPG, (g + 1) * HPG)
                dve.wait_ge(tr_done, n + 1)
                dve.tensor_tensor(heads(xdt[0:L, :], MP), heads(bX[0:L, :], MP),
                                  over_heads(dt_tok[0:L, c, gh], L, MP), ALU.mult).then_inc(xdt_ready, 1)
                dve.tensor_copy(Btok[0:L, :], bM[0:L, 0:P]).then_inc(btok_ready, 1)
                dve.tensor_tensor(Gm[0:L, 0:L], bM[0:L, P:P + L], triu[0:L, c // 4, 0:L], ALU.mult
                                  ).then_inc(g_masked, 1)
                dve.wait_ge(g_masked, n + 1)
                dve.wait_ge(lm_ready, 2 * n + 2)
                dve.tensor_tensor(Lm[0:L, :, 0:L], Lm[0:L, :, 0:L],
                                  Gm[0:L, 0:L].unsqueeze(1).to_broadcast([L, HPG, L]), ALU.mult
                                  ).then_inc(m_ready, 1)
                if g + 1 < MG:
                    conv((g + 1) * GB + 2 * c)
                dve.wait_ge(y_done, n + 1)
                dve.wait_ge(blk_evac, (g + 1) * GB)
                own = bS[:, 0, 0:4 * L]
                yv = yt[:, 0:4 * L]
                if c:
                    dve.wait_ge(e_ready, n + 1)
                    link(dve, "dve", dve.tensor_tensor(yv, bS[:, 1, 0:4 * L], E[:, 0:4 * L], ALU.mult))
                    dve.tensor_tensor(yv, yv, own, ALU.add).then_inc(y_read, 1)
                else:
                    dve.tensor_copy(yv, own).then_inc(y_read, 1)
                dve.wait_ge(y_read, n + 1)
                for j in range(4):
                    last = dve.scalar_tensor_tensor(yt[:, j * L:(j + 1) * L], xg[:, j, tok(c)],
                                                    dsk[:, g * 4 + j:g * 4 + j + 1], yt[:, j * L:(j + 1) * L],
                                                    ALU.mult, ALU.add)
                link(dve, "dve", last)
                yg = y[:, g * 4:g * 4 + 4, tok(c)]
                dve.tensor_tensor(yg, yg, yv.rearrange("p (j l) -> p j l", j=4), ALU.mult).then_inc(y_gated, 1)
                if c == 0:
                    dve.wait_ge(sst_done, states_before(n) + 1)
                    dve.tensor_copy(st[:, g, :], bX[:, :]).then_inc(st_ready, 1)
                elif c < 4:
                    dve.wait_ge(sst_done, states_before(n) + 1)
                    dve.wait_ge(stmp_ready, g * (3 + NB) + c)
                    dve.tensor_tensor(st[:, g, :], bX[:, :], tmp[0], ALU.add).then_inc(st_ready, 1)
                else:
                    for b in range(NB):
                        dve.wait_ge(sst_done, states_before(n) + b + 1)
                        dve.wait_ge(stmp_ready, g * (3 + NB) + 3 + b + 1)
                        dve.tensor_tensor(sdec[:, b, :], (bX, bM)[b % 2][:, :], tmp[b % 2], ALU.add
                                          ).then_inc(st_ready, 1)
                if g + 1 < MG:
                    conv((g + 1) * GB + 2 * c + 1)
                if c == 4:
                    dve.wait_ge(nsq_used, (g + 1) * 4)
                    dve.tensor_scalar(row[:, 0:NP_TOK], bS[:, 0, :], 1.0 / 512, RMS_EPS, ALU.mult, ALU.add)
                    dve.tensor_scalar(row[:, NP_TOK:T], bM[:, 0:ND], 1.0 / 512, RMS_EPS, ALU.mult, ALU.add
                                      ).then_inc(nvar_ready, 1)
                    dve.wait_ge(nroot_ready, g + 1)
                    link(dve, "dve", dve.reciprocal(row[:, :], row[:, :]))
                    for m in range(4 * g, 4 * g + 4):
                        last = dve.scalar_tensor_tensor(y[:, m, :], y[:, m, :], nw[:, m:m + 1], row[:, :],
                                                        ALU.mult, ALU.mult)
                    last.then_inc(y_normed, 1)

            def residual(n_iter, s0, per, b0):
                with dve.Fori(0, n_iter) as i:
                    for j in range(2):
                        dve.wait_ge(w_used, i * (2 * per) + (s0 + (j + 1) * per))
                        xp, xn = xT[:, i * 2 + j, 0:NP_TOK], xT[:, i * 2 + j, NP_TOK:T]
                        dve.scalar_tensor_tensor(xp, xp, ALPHA, bD[j][:, :], ALU.mult, ALU.add)
                        dve.scalar_tensor_tensor(xn, xn, ALPHA, bDn[:, j, 0:ND], ALU.mult, ALU.add
                                                 ).then_inc(blk_evac, 1)

            def layer_norm(k):
                dve.wait_ge(ln_mu, k + 1)
                for m in range(KC):
                    dve.tensor_tensor(xT[:, m, :], xT[:, m, :], row[:, :], ALU.subtract).then_inc(ln_cent, 1)
                dve.wait_ge(ln_used, (k + 1) * KC)
                dve.tensor_scalar(row[:, 0:NP_TOK], bS[:, 0, :], LN_EPS, None, ALU.add)
                dve.tensor_scalar(row[:, NP_TOK:T], bM[:, 0:ND], LN_EPS, None, ALU.add).then_inc(ln_var, 1)
                dve.wait_ge(ln_root, k + 1)
                link(dve, "dve", dve.reciprocal(row[:, :], row[:, :]))
                for m in range(KC):
                    dve.tensor_tensor(xT[:, m, :], xT[:, m, :], row[:, :], ALU.mult).then_inc(ln_scaled, 1)

            def mlp_hidden(k):
                with dve.Fori(0, SL_M1 // NSLOT) as i:
                    for j in range(NSLOT):
                        h = hid[:, i * NSLOT + j, :]
                        dve.wait_ge(w_used, i * NSLOT + (S_M1[k] + j + 1))
                        dve.tensor_scalar(h[:, 0:NP_TOK], bD[j % 2][:, :], 0.0, None, ALU.max)
                        dve.tensor_scalar(h[:, NP_TOK:T], bDn[:, j % 2, 0:ND], 0.0, None, ALU.max
                                          ).then_inc(blk_evac, 1)
                        dve.wait_ge(blk_evac, i * NSLOT + (B_M1[k] + j + 1))
                        dve.tensor_tensor(h, h, h, ALU.mult).then_inc(hid_ready, 1)

            residual(KC // 2, S_OUT, 2, B_OUT)
            layer_norm(0)
            mlp_hidden(0)
            dve.wait_ge(bt_done, 3)
            dve.tensor_copy(bt[:, 0:512], bS[0:NH, 0, :])
            dve.tensor_copy(bt[:, 512:1024], bS[0:NH, 1, :])
            dve.tensor_copy(bt[:, 1024:XN], bX[0:NH, 0:XN - 1024]).then_inc(bt_ready, 1)
            dve.wait_ge(cbt_done, 1)
            flat = cbt.rearrange("p s h -> p (s h)")
            dve.tensor_copy(flat[:, 0:512], bS[:, 0, :])
            dve.tensor_copy(flat[:, 512:NSIG * NH], bS[:, 1, 0:NSIG * NH - 512]).then_inc(cbt_ready, 1)
            residual(KC // 2, S_M2[0], NSLOT, B_M2[0])
            layer_norm(1)

            with dve.Fori(0, SL_KV // NSLOT) as i:
                for j in range(NSLOT):
                    dve.wait_ge(w_used, i * NSLOT + (S_KV + j + 1))
                    dve.tensor_scalar(kvT[:, i * NSLOT + j, 0:NP_TOK], bD[j % 2][:, :], 1.0, None, ALU.mult)
                    dve.tensor_scalar(kvT[:, i * NSLOT + j, NP_TOK:T], bDn[:, j % 2, 0:ND], 1.0, None, ALU.mult
                                      ).then_inc(blk_evac, 1)
            with dve.Fori(0, SL_Q // NSLOT) as i:
                for j in range(NSLOT):
                    dve.wait_ge(w_used, i * NSLOT + (S_Q + j + 1))
                    dve.tensor_scalar(qT[:, i * NSLOT + j, 0:NP_TOK], bD[j % 2][:, :], SCALE, None, ALU.mult)
                    dve.tensor_scalar(qn[:, i, :, j * NS:(j + 1) * NS], by_seq(bDn[:, j % 2, 0:ND]), SCALE, None,
                                      ALU.mult).then_inc(blk_evac, 1)
            dve.wait_ge(gate_exp, 1)
            dve.tensor_scalar(gates[:, 0:4, :], gates[:, 0:4, :], 1.0, None, ALU.add)
            link(dve, "dve", dve.tensor_scalar(gates[0:ND, 4, :], gates[0:ND, 4, :], 1.0, None, ALU.add))
            dve.reciprocal(gates[:, 0:4, :], gates[:, 0:4, :])
            dve.reciprocal(gates[0:ND, 4, :], gates[0:ND, 4, :]).then_inc(gate_ready, 1)
            for c in range(NT):
                dve.wait_ge(vt_done, c + 1)
                dve.tensor_copy(Vt[0:width(c), c, :, :, :].rearrange("p b g d -> p (b g d)"),
                                bS[0:width(c), c % 2, :]).then_inc(vt_ready, 1)
            dve.wait_ge(pe_done, 1)
            dve.tensor_copy(hpe, bX[:, 0:2]).then_inc(hpe_ready, 1)

            def keep_compressed(s_):
                dve.wait_ge(cc_done, s_ + 1)
                dve.tensor_copy(kc[:, s_, :, :].rearrange("p g c -> p (g c)"), bX[:, 0:2 * NCMP])
                dve.tensor_copy(vc[:, s_, :, :].rearrange("p g d -> p (g d)"), bM[0:NCMP, 0:NKV * HD]
                                ).then_inc(cc_ready, 1)

            for s_ in range(NB + 1):
                if s_:
                    keep_compressed(s_ - 1)
                for kv in range(2):
                    dve.wait_ge(ch_done[kv], s_ + 1)
                    if s_ < NB:
                        part = [bS[:, kv, r * P:(r + 1) * P].rearrange("p (t g c) -> p g t c", t=NPG, g=NKV)
                                for r in range(2)]
                        view = lambda v: v.rearrange("p g (t c) -> p g t c", t=NPG)
                    else:
                        part = [bS[:, kv, r * P:(r + 1) * P].rearrange("p (g c) -> p g c", g=NKV)
                                for r in range(2)]
                        view = lambda v: v
                    link(dve, "dve", dve.tensor_copy(view(h1s[kv][:, :, 0:NCMP]), part[1]))
                    dve.tensor_tensor(view(hs[kv]), part[0], view(h1s[kv][:, :, 1:NCMP + 1]), ALU.add
                                      ).then_inc(ch_sum[kv], 1)
            keep_compressed(NB)

            def compressed_probs(qt):
                hc = "p h c -> p (h c)"
                dve.wait_ge(pcs_done, qt + 1)
                s0 = 24 - 8 * qt
                for g in range(NKV):
                    h0 = g * GR
                    src = (bX, bM)[g % 2][:, (g // 2) * P:(g // 2 + 1) * P].rearrange("p (h c) -> p h c", h=GR)
                    last = dve.tensor_tensor(Pc[:, h0:h0 + GR, :], src, cbt[:, s0:s0 + NCMP, h0:h0 + GR]
                                             .rearrange("p s h -> p h s"), ALU.add)
                link(dve, "dve", last)
                link(dve, "dve", dve.tensor_reduce(cmx, Pc, AX.X, ALU.max))
                dve.tensor_tensor(Pc, Pc, cmx.unsqueeze(2).to_broadcast([P, NH, NCMP]), ALU.subtract
                                  ).then_inc(pc_sub, 1)
                dve.wait_ge(pc_exp, qt + 1)
                link(dve, "dve", dve.tensor_reduce(csm, Pc, AX.X, ALU.add))
                link(dve, "dve", dve.reciprocal(csm, csm))
                link(dve, "dve", dve.scalar_tensor_tensor(csm, csm, cvalid[:, qt:qt + 1], gates[:, qt, 0:46:3],
                                                          ALU.mult, ALU.mult))
                dve.tensor_tensor(Pc, Pc, csm.unsqueeze(2).to_broadcast([P, NH, NCMP]), ALU.mult
                                  ).then_inc(pc_ready, 1)

            def maxima(u):
                qt, g, br, _ = ITEMS[u]
                n = (qt + 1) * P
                far = max(n - RB, 0)
                if u >= 2:
                    dve.wait_ge(pv_done, prob_tiles(u - 2)[1])
                for r in range(GR):
                    h = g * GR + r
                    dve.wait_ge(sc_done, GR * u + r + 1)
                    if far:
                        dve.tensor_tensor_reduce(Pb[u % 2][:, r, 0:far], SB[r][:, 0:far],
                                                 Rs[:, h, 0:1].to_broadcast([P, far]), 1.0, -3.0e38,
                                                 ALU.add, ALU.max, mx[:, 0, r:r + 1])
                    last = dve.tensor_tensor_reduce(Pb[u % 2][:, r, far:n], SB[r][:, far:n],
                                                    Rs[:, h, RB - (n - far):RB], 1.0, -3.0e38,
                                                    ALU.add, ALU.max, mx[:, 1, r:r + 1])
                    last.then_inc(sc_read, 1)
                dve.wait_ge(sc_read, GR * (u + 1))
                if far:
                    link(dve, "dve", dve.tensor_tensor(mx[:, 1, :], mx[:, 0, :], mx[:, 1, :], ALU.max))
                dve.tensor_scalar(nmx[:, u % 2, :], mx[:, 1, :], -1.0, None, ALU.mult).then_inc(mx_ready, 1)

            dve.wait_ge(strips_loaded, 16)
            maxima(0)
            for u, (qt, g, br, _) in enumerate(ITEMS):
                if u % 8 == 0:
                    compressed_probs(qt)
                dve.wait_ge(ex_done, u + 1)
                link(dve, "dve", dve.reciprocal(wt[:, u % 2, :], sm[:, u % 2, :]))
                g0 = 12 * g + 1 + br
                dve.tensor_tensor(wt[:, u % 2, :], wt[:, u % 2, :], gates[:, qt, g0:g0 + 10:3], ALU.mult
                                  ).then_inc(wt_ready, 1)
                if u + 1 < len(ITEMS):
                    maxima(u + 1)
                for t in range(*prob_tiles(u)):
                    if t % 2:
                        dve.wait_ge(tp_done[1], t // 2 + 1)
                        if t >= 4:
                            dve.wait_ge(pv_done, t - 3)
                        rows = tile_rows(t)
                        dve.tensor_copy(PT[t % 4][0:rows, :], bM[0:rows, :]).then_inc(pt_ready[1], 1)

            W = PAST + ND

            def new_maxima(b):
                dve.wait_ge(nsc_done, b + 1)
                if b >= 2:
                    dve.wait_ge(ntp_done, b - 1)
                p_ = Pd[b % 2]
                new = bdn[:, b * ND:(b + 1) * ND]
                for i, (lo, hi, bank, bias) in enumerate((
                        (0, PAST, bD[0][:, :], bd), (W, W + PAST, bD[1][:, :], bdw),
                        (2 * W, 2 * W + NCMP, bS[:, 0, 2 * ND:2 * ND + NCMP], bdc),
                        (PAST, W, bS[:, 0, 0:ND], new), (W + PAST, 2 * W, bS[:, 0, ND:2 * ND], new))):
                    last = dve.tensor_tensor_reduce(p_[:, lo:hi], bank, bias, 1.0, -3.0e38, ALU.add, ALU.max,
                                                    dmx[:, i:i + 1])
                last.then_inc(nsc_read, 1)
                dve.wait_ge(nsc_read, b + 1)
                link(dve, "dve", dve.tensor_tensor(dmx[:, 0:2], dmx[:, 0:2], dmx[:, 3:5], ALU.max))
                dve.tensor_scalar(dnm, dmx[:, 0:3], -1.0, None, ALU.mult).then_inc(nmx_ready, 1)

            dve.wait_ge(bd_ready, 1)
            dve.wait_ge(gn_loaded, 16 * NH)
            new_maxima(0)
            for b in range(NB):
                dve.wait_ge(nex_done, b + 1)
                link(dve, "dve", dve.reciprocal(dwt, dsm))
                dve.tensor_tensor(dwt[:, 0:2], dwt[:, 0:2], gn[:, b, 1:3], ALU.mult)
                link(dve, "dve", dve.tensor_tensor(dwt[:, 2:3], dwt[:, 2:3], gn[:, b, 0:1], ALU.mult))
                for i, (lo, hi) in enumerate(((0, W), (W, 2 * W), (2 * W, 2 * W + NCMP))):
                    v = Pd[b % 2][:, lo:hi]
                    last = dve.tensor_scalar(v, v, dwt[:, i:i + 1], None, ALU.mult)
                last.then_inc(npn_ready, 1)
                if b + 1 < NB:
                    new_maxima(b + 1)
                dve.wait_ge(ntp_done, b + 1)
                dve.tensor_copy(PTd[:, PAST:2 * PAST], bM[:, :]).then_inc(npt_dve, 1)

            residual(KC // 2, S_O, 1, B_O)
            layer_norm(2)
            dve.wait_ge(outs, 64)
            mlp_hidden(1)
            residual(KC // 2, S_M2[1], NSLOT, B_M2[1])
            layer_norm(3)


def slots(w):
    K, M = w.shape
    v = w.reshape(K // D, KC, P, M // P, P)
    return v.transpose(3, 0, 2, 1, 4).reshape(-1, P, SLOT)


def feat(v):
    v = v.reshape(*v.shape[:-1], -1, P)
    return np.moveaxis(v, -1, 0)


def kernel(**inputs):
    import numpy as _np
    import concourse.bacc as _bacc
    from concourse import mybir as _mybir
    from concourse.bass_utils import run_bass_kernel_spmd as _run

    x = {k: _np.asarray(v) for k, v in inputs.items()}
    A = {}
    A["x"] = feat(_np.concatenate([x["x_prompt"].reshape(NP_TOK, D), x["x_sample"].reshape(ND, D)]))\
        .transpose(0, 2, 1)
    win = x["m_in_w"][0]
    z, xs, Bw, Cw, dtw = _np.split(win, [DI, 2 * DI, 2 * DI + 512, 2 * DI + 1024], axis=1)
    order = []
    for g in range(MG):
        order += [xs[:, g * 512:(g + 1) * 512], Bw[:, g * P:(g + 1) * P], Cw[:, g * P:(g + 1) * P],
                  z[:, g * 512:(g + 1) * 512]]
    A["w"] = _np.concatenate([slots(_np.concatenate(order, axis=1)), slots(x["m_out_w"][0]),
                              slots(x["mlp_w1"][0]), slots(x["mlp_w2"][0]), slots(x["kv_w"]),
                              slots(q_columns(x["q_w"][0])), slots(o_rows(x["o_w"][0])),
                              slots(x["mlp_w1"][1]), slots(x["mlp_w2"][1])])
    A["dtw"] = dtw.reshape(KC, P, MH).transpose(1, 0, 2)
    A["dtb"] = _np.stack([x["m_dt_bias"][0], x["m_a_log"][0]], axis=1)

    def conv_order(v):
        a_, b_, c_ = _np.split(v, [DI, DI + 512], axis=-1)
        parts = []
        for g in range(MG):
            parts += [a_[..., g * 512:(g + 1) * 512], b_[..., g * P:(g + 1) * P], c_[..., g * P:(g + 1) * P]]
        return feat(_np.concatenate(parts, axis=-1))

    A["cst"] = conv_order(x["state_conv"][0]).transpose(0, 3, 1, 2)
    A["cw"] = conv_order(x["m_conv_w"][0]).transpose(0, 2, 1)
    A["cb"] = conv_order(x["m_conv_b"][0])
    A["nw"] = feat(x["m_norm_w"][0])
    A["dsk"] = feat(_np.broadcast_to(x["m_d"][0][:, None], (MH, MP)).reshape(-1))
    A["lng"] = feat(x["ln_g"].reshape(4, D))
    A["lnb"] = feat(x["ln_b"].reshape(4, D))
    A["state"] = x["state_ssm"][0].transpose(0, 3, 1, 2).reshape(NB, MN, DI)
    t = _np.arange(P)
    seq = _np.arange(ND) // NS
    same = _np.zeros((P, P), bool)
    same[:ND, :ND] = seq[:, None] == seq[None, :]
    upper = t[:, None] <= t[None, :]
    A["triu"] = _np.stack([upper, upper & same], axis=1).astype(_np.float32)
    A["low"] = _np.stack([~upper, ~upper & same], axis=1).astype(_np.float32)
    A["ident"] = _np.eye(P, dtype=_np.float32)
    A["smask"] = (seq[:, None] == _np.arange(NB)[None, :]).astype(_np.float32)
    outs = {"o_pssm": (P, DI), "o_sssm": (NB, MN, DI), "o_pconv": (P, NXB, 3), "o_sconv": (P, NXB, NB, 3)}
    attention_layout(A, outs, x)

    nc = _bacc.Bacc("TRN2", target_bir_lowering=False, num_devices=1)
    dev = {}
    for name, v in A.items():
        A[name] = v = _np.ascontiguousarray(v)
        dev[name] = nc.dram_tensor("in_" + name, v.shape, _mybir.dt.from_np(v.dtype), kind="ExternalInput").ap()
    for name, shape in (("gscr", (ND, 3 * NH)), ("bscr", (NH, XN)), ("bskew", (P, NH, RW))):
        dev[name] = nc.dram_tensor(name, shape, F32, kind="Internal").ap()
    for name, shape in outs.items():
        dev[name] = nc.dram_tensor(name, shape, F32, kind="ExternalOutput").ap()
    build(nc, dev)
    r = _run(nc, [{"in_" + name: v for name, v in A.items()}], core_ids=[0]).results[0]
    return finish(r)


def q_columns(w):
    return w[:, :D].reshape(D, 2, 2, GR, HD).transpose(0, 1, 3, 2, 4).reshape(D, D)


def o_rows(w):
    return w.reshape(2, 2, GR, HD, D).transpose(0, 2, 1, 3, 4).reshape(D, D)


def kv_rows(c):
    lead = c.shape[:-4]
    k = c[..., 0, :, :].reshape(*lead, PAGE, 2, P)
    k = np.moveaxis(k, -1, -3)
    k = np.swapaxes(k, -1, -2).reshape(*lead, P, 256)
    v = c[..., 1, :, :].reshape(*lead, PAGE, 256)
    return np.concatenate([k, v], axis=-1)


def kv_rows_back(r):
    lead = r.shape[:-2]
    k = np.swapaxes(r[..., 0:256].reshape(*lead, P, 2, PAGE), -1, -2)
    k = np.moveaxis(k, -3, -1).reshape(*lead, PAGE, NKV, HD)
    v = r[..., 256:512].reshape(*lead, PAGE, NKV, HD)
    return np.stack([k, v], axis=-3)


def bucket(dist):
    n = np.maximum(dist, 16).astype(np.float64)
    large = 16 + np.floor(np.log(n / 16) / np.log(8.0) * 16 + 1e-9).astype(int)
    return np.where(dist < 0, NBK, np.where(dist < 16, np.maximum(dist, 0), np.minimum(large, NBK - 1)))


def attention_layout(A, outs, x):
    f32 = np.float32
    rows = np.arange(NBK + 1)[:, None]
    A["eb"] = (rows == bucket(Y0 - np.arange(XN))[None, :]).astype(f32)
    A["ef"] = (rows == bucket(np.arange(XN) - X0)[None, :]).astype(f32)
    A["relb"] = x["rel_bias"]
    A["gw"] = x["q_w"][0][:, D:].reshape(KC, P, 3 * NH).transpose(1, 0, 2)
    A["cw1"] = x["cmp_w1"].reshape(2, 2, 8, P, P).transpose(3, 0, 1, 2, 4)
    A["cw2"] = x["cmp_w2"].transpose(1, 0, 2)
    A["cpe"] = x["cmp_pe"].reshape(2, 2, 8, P).transpose(3, 0, 1, 2)
    q = np.arange(NP_TOK)
    A["cvalid"] = (q >= CL - 1).astype(f32).reshape(4, P).T
    i = np.arange(P) % NS
    A["wmask"] = np.where(np.arange(NS)[None, :] <= i[:, None], NEG, 0.0).astype(f32)
    A["ptab"] = x["page_table"].reshape(1, NB * NPG)
    A["sel"] = kv_rows(x["cache_sel_kv"])
    A["win"] = kv_rows(x["cache_win_kv"].reshape(NB, NPG, PAGE, 2, NKV, HD)).transpose(0, 2, 1, 3)
    A["cmp"] = x["cache_cmp_kv"].reshape(NPHYS, 8, 8, 2, 2, NKV, HD).transpose(0, 3, 6, 4, 2, 5, 1)\
        .reshape(NPHYS, P, 512)
    outs.update(o_kv=(P, 12, T), o_win=(NB, P, NPG, 512), o_y=(P, KC, T))


def finish(r):
    def tokens(v):
        return np.ascontiguousarray(np.asarray(v).transpose(2, 1, 0)).reshape(v.shape[2], -1)

    y = tokens(r["o_y"])
    kv = tokens(r["o_kv"]).reshape(T, 3, 2, NKV, HD)
    new = kv[NP_TOK:].reshape(NB, NS, 3, 2, NKV, HD)
    win = kv_rows_back(np.asarray(r["o_win"]).transpose(0, 2, 1, 3)).reshape(NB, PAST, 2, NKV, HD)
    p_ssm = np.asarray(r["o_pssm"]).reshape(MN, MH, MP).transpose(1, 2, 0)[None, None]
    s_ssm = np.asarray(r["o_sssm"]).reshape(NB, MN, MH, MP).transpose(0, 2, 3, 1)[None]

    def conv_rows(v):
        v = np.moveaxis(np.asarray(v), (1, 0), (-2, -1))
        v = v.reshape(*v.shape[:-2], MG, XB, P)
        lead = v.shape[:-3]
        return np.concatenate([v[..., 0:4, :].reshape(*lead, DI), v[..., 4, :].reshape(*lead, MG * P),
                               v[..., 5, :].reshape(*lead, MG * P)], axis=-1)

    p_conv = conv_rows(r["o_pconv"])[None, None]
    s_conv = conv_rows(r["o_sconv"])[None]
    out = (y[:NP_TOK].reshape(1, NP_TOK, D), y[NP_TOK:].reshape(NB, NS, D), p_ssm, p_conv,
           kv[None, :NP_TOK, 0], kv[None, :NP_TOK, 1], kv[None, :NP_TOK, 2],
           s_ssm, s_conv, new[:, :, 0], new[:, :, 1], np.concatenate([win[:, NS:], new[:, :, 2]], axis=1))
    return tuple(np.ascontiguousarray(v) for v in out)
```

```python
from contextlib import ExitStack

import numpy as np

import concourse.bass as bass
from concourse import mybir

F32 = mybir.dt.float32
F32R = mybir.dt.float32r
I32 = mybir.dt.int32
ALU = mybir.AluOpType
ACT = mybir.ActivationFunctionType
AX = mybir.AxisListType

P = 128
D = 1024
KC = D // P
NP_TOK = 512
NB, NS = 8, 8
ND = NB * NS
T = NP_TOK + ND
HT = T // 2
NPB = NP_TOK - HT
PAST = 512
PAGE = 128
NPG = PAST // PAGE
NPHYS = NB * NPG + NB * NPG // 4
DI = 2 * D
MH, MP, MN, MG = 32, 64, 128, 4
HPG = MH // MG
GB = 10
XB = 6
NXB = MG * XB
CONV = 4
NH, NKV, HD = 16, 4, 64
GR = NH // NKV
DFF = 4 * D
NBK = 32
NCMP = 32
CL, CS = 32, 16
ALPHA = 4.0 ** 0.25
LN_EPS = 1e-5
RMS_EPS = 1e-5
SCALE = float(HD) ** -0.5
NEG = -1e30
Y0 = 527
X0 = 527
CB0 = 353
NSIG = 56
XN = 1040
ARENA = 44000
SLOT = KC * P
NSLOT = 2
NT = 5
RB = 256
RW = 384

SL_IN = MG * GB
SL_OUT = KC * 2
SL_M1 = DFF // P
SL_M2 = KC * 4
SL_KV = 12
SL_Q = 8
SL_O = 8
N_SLOTS = SL_IN + SL_OUT + SL_M1 + SL_M2 + SL_KV + SL_Q + SL_O + SL_M1 + SL_M2


def build(nc, a):
    with ExitStack() as ctx:
        def sb(name, shape, dt=F32):
            return ctx.enter_context(nc.sbuf_tensor(name, shape, dt))

        def sem(name):
            return ctx.enter_context(nc.semaphore(name))

        dense = ctx.enter_context(nc.psum_tensor("dense", [P, 4, 512], F32))
        bD = [dense[:, 0, :], dense[:, 1, :]]
        bDn = dense[:, 2:4, :]
        bX = ctx.enter_context(nc.psum_tensor("bX", [P, 512], F32))
        bM = ctx.enter_context(nc.psum_tensor("bM", [P, 512], F32))
        bS = ctx.enter_context(nc.psum_tensor("bS", [P, 2, 512], F32))

        ring = sb("ring", [P, NSLOT, SLOT])
        split = sb("split", [P, NSLOT, 2, SLOT], F32R)
        ident = sb("ident", [P, P])
        triu = sb("triu", [P, 2, P])
        low = sb("low", [P, 2, P])
        ones = sb("ones", [P, P])
        onesd = sb("onesd", [P, P])
        lng = sb("lng", [P, 4, KC])
        lnb = sb("lnb", [P, 4, KC])
        row = sb("row", [P, T])
        sq = sb("sq", [P, 2, T])
        arena = sb("arena", [P, ARENA])
        at = [0]

        arena_at = nc.sbuf_base - 4 * ARENA
        tiles = []

        def carve(*shape, parts=P):
            first = at[0]
            at[0] += int(np.prod(shape))
            assert at[0] <= ARENA, at[0]
            tiles.append(nc.alloc_sbuf_tensor_at(f"tile{len(tiles)}", [parts, *shape], F32,
                                                 offset=arena_at + 4 * first, align_bytes=4))
            return tiles[-1][tuple(slice(0, n) for n in (parts, *shape))]

        def split_tile(name, first, *shape):
            return nc.alloc_sbuf_tensor_at(name, [P, *shape], F32R, offset=arena_at + 4 * first, align_bytes=4)

        xT = carve(KC, T)
        at[0] = 2 * (3 + NP_TOK + NB * (3 + NS)) + 2 * T + XB * T
        assert at[0] >= KC * T
        xs_at = at[0]
        xs = split_tile("xs", xs_at, 2, KC, T)
        xs_end = xs_at + 2 * KC * T

        at[0] = 0
        raw = [carve(3 + NP_TOK + NB * (3 + NS)) for _ in range(2)]
        acc = [carve(T) for _ in range(2)]
        xbc = [carve(XB, T)]
        assert at[0] == xs_at
        at[0] = xs_end
        xbc.append(carve(XB, T))
        y = carve(DI // P, T)
        y_lo = split_tile("y_lo", at[0] - DI // P * T, DI // P, T)
        y_hi = xs.rearrange("p s k t -> p (s k) t")
        at[0] = xs_end
        dtT = carve(T, parts=MH)
        dw = [carve(T, parts=MH) for _ in range(4)]
        aT = carve(T, parts=MH)
        at[0] = xs_end + (XB + DI // P) * T
        cst = carve(NXB, NB, 3)
        lastp = carve(NXB, 3)
        lastd = cst
        cw = carve(NXB, CONV)
        cb = carve(NXB)
        nw = carve(DI // P)
        dsk = carve(DI // P)
        dtw = carve(KC, MH)
        dtb = carve(2, parts=MH)
        smask = carve(NB, parts=ND)
        dt_tok = carve(NT, MH)
        a_tok = carve(NT, MH)
        dec_tok = carve(NT, MH)
        tot = carve(4, MH)
        totd = carve(NB, MH)
        am = carve(NB, MH, parts=ND)
        AH = carve(HPG, P)
        AR = carve(HPG * MP)
        Lm = carve(HPG, P)
        Gm = carve(P)
        E = carve(512)
        xdt = carve(HPG * MP)
        xdec = carve(HPG * MP)
        Btok = carve(P)
        Bm = carve(NB, P, parts=ND)
        st = carve(MG, HPG * MP)
        tmp = [carve(HPG * MP) for _ in range(2)]
        yt = carve(512)
        sdec = carve(NB, HPG * MP)
        mamba_end = at[0]

        hid = split_tile("hid", xs_end, 2, DFF // P // 2, T)
        hid_end = xs_end + DFF // P * T

        at[0] = xs_end
        kvT = carve(12, T)
        qT = carve(8, T)
        qn = carve(2, NB, GR * NS)
        Vt = carve(NT, 2, NKV, HD)
        kc = carve(NB + 1, 2, NCMP)
        vc = carve(NB + 1, NKV, HD, parts=NCMP)
        gates = carve(NT, 3 * NH)
        gn = carve(NB, 3)
        mx, nmx, sm, wt = carve(2, 4), carve(2, 4), carve(2, 4), carve(2, 4)
        SB = [bD[0], bD[1], bS[:, 0, :], bS[:, 1, :]]
        cmx, csm = carve(NH), carve(NH)
        dmx, dnm, dsm, dwt = carve(5), carve(3), carve(3), carve(3)
        assert at[0] <= hid_end
        PT = [kvT[:, i, 0:512] for i in range(4)]
        at[0] = KC * T
        bd = carve(512)
        bdw = carve(512)
        nr = carve(P + NS * 2)
        assert at[0] <= xs_at
        at[0] = hid_end
        cw1 = carve(2, 2, 8, P)
        at[0] = hid_end
        ef = carve(XN, parts=NBK + 1)
        eb = carve(XN, parts=NBK + 1)
        bt = carve(XN, parts=NH)
        at[0] = hid_end
        kv0 = [carve(NPG, 512) for _ in range(2)]
        relb = carve(NH, parts=NBK + 1)
        cw2 = carve(2, HD)
        cpe = carve(2, 2, 8)
        hpe = carve(2)
        h1s = [carve(NKV, NCMP + 1) for _ in range(2)]
        gw = carve(KC, 3 * NH)
        cbt = carve(NSIG, NH)
        cvalid = carve(4)
        bdn = carve(NB * 72)
        bdc = carve(NCMP)
        FARC = (PAST - P - CL + 1) // CS + 1
        wmask = carve(NS)
        Rs = carve(NH, RB)
        at[0] = xs_at
        Pb = [carve(GR, NP_TOK) for _ in range(2)]
        ct = [carve(NPG, 512) for _ in range(2)]
        Pc = carve(NH, NCMP)
        hs = [carve(NKV, NCMP) for _ in range(2)]
        assert at[0] <= xs_end
        skv = [kv0[0], ct[0]]
        wkv = [kv0[1], ct[1]]
        at[0] = xs_at
        zx = carve(4, 256)
        tp = carve(2, NKV, 8, NCMP)
        at[0] = xs_at
        Pd = [carve(2 * (PAST + ND) + NCMP) for _ in range(2)]
        PTd = carve(2 * PAST)
        PTs = carve(3 * P)
        assert at[0] <= xs_at + 2 * GR * NP_TOK
        ptab = sb("ptab", [1, NB * NPG], I32)

        H1, H2 = SL_M1 // 2, SL_M2 // 2
        S_OUT = (SL_IN, SL_IN + KC)
        S_M1, S_M2, s0 = [], [], SL_IN + SL_OUT
        B_OUT = (SL_IN, SL_IN + KC)
        B_M1, B_M2, b0 = [], [], SL_IN + 2 * KC
        for layer in range(2):
            S_M1.append((s0, s0 + H1 + H2))
            S_M2.append((s0 + H1, s0 + 2 * H1 + H2))
            s0 += 2 * (H1 + H2)
            B_M1.append((b0, b0 + H1 + KC))
            B_M2.append((b0 + H1, b0 + 2 * H1 + KC))
            b0 += 2 * (H1 + KC)
            if layer == 0:
                S_KV, B_KV = s0, b0
                S_Q, B_Q = s0 + SL_KV, b0 + SL_KV
                S_O, B_O = S_Q + SL_Q, B_Q + SL_Q
                s0, b0 = S_O + SL_O, B_O + KC
        assert s0 == N_SLOTS

        PARAM_TILES = ((dtw, "dtw"), (dtb, "dtb"), (ident[:, :], "ident"), (triu[:, :, :], "triu"),
                       (low[:, :, :], "low"), (smask, "smask"), (cst, "cst"), (cw, "cw"), (cb, "cb"),
                       (nw, "nw"), (dsk, "dsk"), (lng[:, :, :], "lng"), (lnb[:, :, :], "lnb"))
        N_PARAMS = len(PARAM_TILES)

        ATT_TILES = ((eb, "eb"), (ef, "ef"), (gw, "gw"), (cw2, "cw2"), (cpe, "cpe"),
                     (cvalid, "cvalid"), (wmask, "wmask"))
        N_ATT = 1 + len(ATT_TILES)
        s_x = sem("x_loaded")
        s_dtw = sem("dt_weights_loaded")
        s_par = sem("params_loaded")
        x_back = sem("x_loaded_again")
        w_ready = [sem(f"slot_loaded{i}") for i in range(NSLOT)]
        w_hi = sem("slots_hi")
        w_split = sem("slots_split")
        w_used = sem("slots_used")
        x_hi = sem("stream_hi")
        x_split = sem("stream_split")
        y_his = sem("y_hi")
        y_split = sem("y_split")
        y_split_last = sem("y_split_last_group")
        o_hi = sem("o_hi")
        o_split = sem("o_split")
        hid_sq = sem("hidden_squared")
        hid_hi = sem("hidden_hi")
        blk_evac = sem("block_evacuated")
        dve_step = sem("dve_step")
        act_step = sem("act_step")
        s_const = sem("constants_set")
        raw_zeroed = sem("rows_before_the_prompt_zeroed")
        dt_done = sem("dt_projected")
        dt_abs = sem("dt_exp_ready")
        dt_ready = sem("dt_and_a_ready")
        dt_tr = sem("dt_transposed")
        dt_tok_ready = sem("dt_by_token")
        am_ready = sem("a_by_sequence")
        dec_sum = sem("decay_sums")
        dec_ready = sem("decays_ready")
        conv_done = sem("conv_summed")
        xbc_ready = sem("xbc_ready")
        ah_ready = sem("segment_rows_ready")
        tr_done = sem("x_b_and_cb_summed")
        seg_done = sem("segment_sums")
        ac_done = sem("running_sums")
        btok_ready = sem("b_by_token")
        lm_ready = sem("segment_decays")
        e_ready = sem("running_decays")
        xdt_ready = sem("xdt_ready")
        g_masked = sem("cb_masked")
        m_ready = sem("mix_ready")
        xdec_ready = sem("xdec_ready")
        y_done = sem("y_summed")
        y_read = sem("y_banks_read")
        y_gated = sem("y_gated")
        sst_done = sem("state_summed")
        stmp_ready = sem("state_decayed")
        st_ready = sem("state_ready")
        bm_ready = sem("b_by_sequence")
        sd_loaded = sem("old_states_loaded")
        sd_stored = sem("new_states_stored")
        nsq_ready = sem("y_squared")
        nsq_used = sem("y_squares_summed")
        nvar_ready = sem("y_variance")
        nroot_ready = sem("y_root")
        y_normed = sem("y_normed")
        ln_mean = sem("ln_mean_summed")
        ln_mu = sem("ln_mean_ready")
        ln_cent = sem("ln_centered")
        ln_sq = sem("ln_squared")
        ln_used = sem("ln_squares_summed")
        ln_var = sem("ln_variance")
        ln_root = sem("ln_root")
        ln_scaled = sem("ln_scaled")
        x_ready = sem("stream_ready")
        hid_ready = sem("hidden_ready")
        outs = sem("outputs_stored")

        x_out = sem("result_stored")
        s_tab = sem("attention_params_loaded")
        s_cw1 = sem("cw1_loaded")
        s_ptab = sem("page_table_loaded")
        negb_set = sem("mask_row_set")
        bt_done = sem("bias_table_summed")
        bt_ready = sem("bias_table_ready")
        bt_stored = sem("bias_table_stored")
        skew_stored = sem("bias_rows_repeated")
        rows_loaded = sem("new_bias_rows_loaded")
        strips_loaded = sem("bias_strips_loaded")
        bd_ready = sem("new_bias_ready")
        cbt_done = sem("compressed_bias_summed")
        cbt_ready = sem("compressed_bias_ready")
        gate_done = sem("gates_summed")
        gate_exp = sem("gates_exp")
        gate_ready = sem("gates_ready")
        gate_stored = sem("gates_stored")
        gn_loaded = sem("new_gates_loaded")
        vt_done = sem("v_transposed")
        vt_ready = sem("v_by_token")
        ct_loaded = [sem(f"compression_rows{i}") for i in range(2)]
        zx_ready = sem("crossing_rows_ready")
        tp_ready = sem("own_half_rows_ready")
        tp_loaded = sem("crossed_rows_loaded")
        pe_done = sem("position_sums")
        hpe_ready = sem("position_bias_ready")
        ch_done = [sem(f"compress_hidden{i}") for i in range(2)]
        ch_sum = [sem(f"compress_hidden_added{i}") for i in range(2)]
        ch_ready = [sem(f"compress_hidden_ready{i}") for i in range(2)]
        cc_done = sem("compressed_summed")
        cc_ready = sem("compressed_ready")
        pcs_done = sem("compressed_scores")
        pc_sub = sem("compressed_scores_shifted")
        pc_exp = sem("compressed_exp")
        pc_ready = sem("compressed_probs")
        sc_done = sem("scores_done")
        sc_read = sem("scores_read")
        mx_ready = sem("maxima_ready")
        ex_done = sem("exp_done")
        wt_ready = sem("weights_ready")
        pn_ready = sem("probs_ready")
        tp_done = [sem(f"probs_transposed{i}") for i in range(2)]
        pt_ready = [sem(f"probs_by_key{i}") for i in range(2)]
        pv_done = sem("probs_used")
        o_ready = sem("o_ready")
        kv_loaded = [sem(f"cache_rows_loaded{i}") for i in range(2)]
        win_stored = [sem(f"window_rows_stored{i}") for i in range(2)]
        nsc_done = sem("new_scores_done")
        nsc_read = sem("new_scores_read")
        nmx_ready = sem("new_maxima_ready")
        nex_done = sem("new_exp_done")
        npn_ready = sem("new_probs_ready")
        ntp_done = sem("new_probs_transposed")
        npt_act = sem("new_probs_by_key_a")
        npt_dve = sem("new_probs_by_key_b")
        no_done = sem("new_o_summed")
        no_ready = sem("new_o_ready")

        block = ctx.enter_context(nc.Block())
        steps = {"dve": 0, "act": 0}

        def link(eng, who, ins):
            s = dve_step if who == "dve" else act_step
            ins.then_inc(s, 1)
            steps[who] += 1
            eng.wait_ge(s, steps[who])

        def width(c):
            return P if c < 4 else ND

        def tok(c):
            return slice(c * P, c * P + width(c))

        def by_seq(v):
            return v.rearrange("p (b i) -> p b i", b=NB)

        def heads(v, d):
            return v.rearrange("p (h d) -> p h d", d=d)

        def over_heads(v, L, n):
            return v.unsqueeze(2).to_broadcast([L, HPG, n])

        def at_step(v, i, step):
            return v if i is None else i * step + v

        def halves(v):
            return v.rearrange("p (h n) -> p h n", h=2)

        def dense_out(par):
            return dense[:, 2 * par:2 * par + 2, 0:HT]

        stat = bS[:, :, 0:HT]

        def states_before(n):
            g, c = divmod(n, NT)
            return g * (4 + NB) + c

        ITEMS = []
        for qt in range(4):
            for g in range(NKV):
                for br in range(2):
                    ITEMS.append((qt, g, br, len(ITEMS)))

        def prob_tiles(u):
            t0 = sum(qt + 1 + (br == 0) for qt, _, br, _ in ITEMS[:u])
            return t0, t0 + ITEMS[u][0] + 1 + (ITEMS[u][2] == 0)

        COMPRESSED_TILES = {prob_tiles(u)[0] for _, _, br, u in ITEMS if br == 0}

        def tile_rows(t):
            return NCMP if t in COMPRESSED_TILES else P

        def half_of(g):
            return slice((g % 2) * HD, (g % 2) * HD + HD)

        def filler(g, c):
            if g + 1 < MG:
                s = (g + 1) * GB + 2 * c
            elif c:
                s = S_OUT[0] + 2 * (c - 1)
            else:
                return ()
            return s, s + 1

        TILES = [(g, c, g * NT + c) for g in range(MG) for c in range(NT)]

        def raw_new(j):
            return raw[j][:, 3 + NP_TOK:].rearrange("p (b i) -> p b i", b=NB)

        @block.sync
        def _(sp):
            for j in range(NSLOT):
                sp.dma_start(ring[:, j, :], a["w"][j, :, :]).then_inc(w_ready[j], 16)

            def stream(first, last):
                with sp.Fori(first // NSLOT, last // NSLOT) as i:
                    for j in range(NSLOT):
                        sp.wait_ge(w_split, i * NSLOT + (j + 1 - NSLOT))
                        sp.dma_start(ring[:, j, :], a["w"][i * NSLOT + j, :, :]).then_inc(w_ready[j], 16)

            stream(NSLOT, S_OUT[0] + 2 * NSLOT)
            sp.wait_ge(xbc_ready, NXB)
            sp.wait_ge(y_gated, (MG - 1) * NT)
            sp.dma_start(xT, a["x"]).then_inc(x_back, 16)
            s_bias = S_M2[0][0] + 2 * NSLOT
            stream(S_OUT[0] + 2 * NSLOT, s_bias)
            sp.wait_ge(bt_ready, 1)
            sp.dma_start(a["bscr"], bt).then_inc(bt_stored, 16)
            stream(s_bias, s_bias + NSLOT)
            y0 = Y0 - 2 * P + 1
            sp.wait_ge(bt_stored, 16)
            sp.dma_start(a["bskew"], bass.AP(a["bscr"].tensor, y0, [[0, P], [XN, NH], [1, RW]])
                         ).then_inc(skew_stored, 16)
            stream(s_bias + NSLOT, s_bias + 2 * NSLOT)
            sp.wait_ge(skew_stored, 16)
            sp.dma_start(Rs, bass.AP(a["bskew"].tensor, P - 1, [[NH * RW - 1, P], [RW, NH], [1, RB]])
                         ).then_inc(strips_loaded, 16)
            stream(s_bias + 2 * NSLOT, s_bias + 3 * NSLOT)
            sp.wait_ge(strips_loaded, 16)
            for h in range(NH):
                sp.dma_start(nr[h * NS:(h + 1) * NS, :], Rs[0:NS, h, 0:P + 2 * NS]).then_inc(rows_loaded, 16)
            stream(s_bias + 3 * NSLOT, S_O + 2 * NSLOT)
            sp.wait_ge(s_ptab, 16)
            sp.wait_ge(cc_ready, NB + 1)
            for b in range(NB):
                if b >= 2:
                    sp.wait_ge(no_done, b - 1)
                    sp.wait_ge(win_stored[b % 2], 16 * (b // 2))
                for pg in range(NPG):
                    page = sp.value_load(ptab[0:1, b * NPG + pg:b * NPG + pg + 1], min_val=0, max_val=NPHYS - 1)
                    sp.dma_start(skv[b % 2][:, pg, :], a["sel"][page, :, :]).then_inc(kv_loaded[b % 2], 16)
                sp.dma_start(wkv[b % 2], a["win"][b, :, :, :]).then_inc(kv_loaded[b % 2], 16)
            stream(S_O + 2 * NSLOT, N_SLOTS)

        @block.gpsimd
        def _(pool):
            pool.memset(ones[:, :], 1.0)
            pool.memset(onesd[:, :], 1.0 / D).then_inc(s_const, 1)

            def load_states(g):
                if g:
                    pool.wait_ge(sd_stored, 16 * g)
                pool.dma_start(sdec, a["state"][:, :, g * 512:(g + 1) * 512]
                               .rearrange("b n m -> n b m")).then_inc(sd_loaded, 16)

            def segment_rows(g, c, n):
                L = width(c)
                if n:
                    pool.wait_ge(ac_done, n)
                pool.tensor_copy(heads(AR[0:L, :], MP), over_heads(a_tok[0:L, c, g * HPG:(g + 1) * HPG], L, MP))
                pool.tensor_tensor(AH[0:L, :, 0:L],
                                   low[0:L, c // 4, 0:L].unsqueeze(1).to_broadcast([L, HPG, L]),
                                   over_heads(a_tok[0:L, c, g * HPG:(g + 1) * HPG], L, L),
                                   ALU.mult).then_inc(ah_ready, 1)

            def split_lo(s, i=None):
                pool.wait_ge(w_hi, at_step(s + 1, i, NSLOT))
                j = s % NSLOT
                pool.tensor_tensor(split[:, j, 1, :], ring[:, j, :], split[:, j, 0, :].bitcast(F32),
                                   ALU.subtract).then_inc(w_split, 1)

            def split_los(first, last):
                with pool.Fori(0, (last - first) // NSLOT) as i:
                    for j in range(NSLOT):
                        split_lo(first + j, i)

            def y_los(first, last):
                for m in range(first, last):
                    pool.wait_ge(y_his, m + 1)
                    pool.tensor_tensor(y_lo[:, m, :], y[:, m, :], y_hi[:, m, :].bitcast(F32), ALU.subtract
                                       ).then_inc(y_split, 1)

            split_lo(0)
            split_lo(1)
            load_states(0)
            pool.wait_ge(dt_done, 1)
            pool.wait_ge(x_split, KC)
            pool.memset(raw[0][:, 0:3], 0.0)
            pool.memset(raw[1][:, 0:3], 0.0).then_inc(raw_zeroed, 1)
            pool.wait_ge(s_par, 16 * (N_PARAMS - 1))
            pool.wait_ge(dt_tok_ready, 1)
            pool.tensor_tensor(am, a_tok[0:ND, 4, :].unsqueeze(1).to_broadcast([ND, NB, MH]),
                               smask.unsqueeze(2).to_broadcast([ND, NB, MH]), ALU.mult).then_inc(am_ready, 1)
            pool.wait_ge(dec_ready, 1)
            segment_rows(0, 0, 0)
            for s_ in range(2, GB + 2):
                split_lo(s_)
            for g, c, n in TILES:
                L = width(c)
                pool.wait_ge(xdt_ready, n + 1)
                pool.tensor_tensor(heads(xdec[0:L, :], MP), heads(xdt[0:L, :], MP),
                                   over_heads(dec_tok[0:L, c, g * HPG:(g + 1) * HPG], L, MP),
                                   ALU.mult).then_inc(xdec_ready, 1)
                if c == 4:
                    pool.wait_ge(btok_ready, n + 1)
                    pool.tensor_tensor(Bm, Btok[0:ND, :].unsqueeze(1).to_broadcast([ND, NB, P]),
                                       smask.unsqueeze(2).to_broadcast([ND, NB, P]), ALU.mult
                                       ).then_inc(bm_ready, 1)
                if n + 1 < len(TILES):
                    segment_rows(*TILES[n + 1])
                if g == MG - 1:
                    if c == 0:
                        y_los(0, 8)
                    if c == 1:
                        y_los(8, 12)
                if filler(g, c):
                    split_lo(filler(g, c)[0] + 2)
                if 1 <= c < 4:
                    pool.wait_ge(st_ready, states_before(n))
                    pool.tensor_tensor(heads(tmp[0], MP), heads(st[:, g, :], MP),
                                       over_heads(tot[:, c, g * HPG:(g + 1) * HPG], P, MP),
                                       ALU.mult).then_inc(stmp_ready, 1)
                if c == 4:
                    pool.wait_ge(sd_loaded, 16 * (g + 1))
                    for b in range(NB):
                        pool.wait_ge(st_ready, states_before(n) + max(b - 1, 0))
                        pool.tensor_tensor(heads(tmp[b % 2], MP), heads(sdec[:, b, :], MP),
                                           over_heads(totd[:, b, g * HPG:(g + 1) * HPG], P, MP),
                                           ALU.mult).then_inc(stmp_ready, 1)
                    pool.wait_ge(st_ready, states_before(n) + NB)
                    pool.dma_start(a["o_sssm"][:, :, g * 512:(g + 1) * 512].rearrange("b n m -> n b m"),
                                   sdec).then_inc(sd_stored, 16)
                    if g + 1 < MG:
                        load_states(g + 1)
                if filler(g, c):
                    split_lo(filler(g, c)[1] + 2)
            pool.dma_start(a["o_pssm"], st.rearrange("p g m -> p (g m)")).then_inc(outs, 16)
            pool.wait_ge(conv_done, NXB)
            pool.dma_start(a["o_pconv"], lastp).then_inc(outs, 16)
            pool.dma_start(a["o_sconv"], lastd).then_inc(outs, 16)
            split_los(S_OUT[1] + 2, S_M1[0][0] + 2)
            pool.wait_ge(sd_stored, 16 * MG)
            pool.wait_ge(outs, 48)

            def x_los(k):
                for m in range(KC):
                    pool.wait_ge(x_ready, k * KC + m + 1)
                    pool.tensor_tensor(xs[:, 1, m, :], xT[:, m, :], xs[:, 0, m, :].bitcast(F32), ALU.subtract
                                       ).then_inc(x_split, 1)

            def mlp_los(k, half, end):
                with pool.Fori(0, H1 // NSLOT) as i:
                    for j in range(NSLOT):
                        split_lo(S_M1[k][half] + 2 + j, i)
                        pool.wait_ge(hid_hi, i * NSLOT + ((2 * k + half) * H1 + j + 1))
                        m = i * NSLOT + j
                        pool.tensor_tensor(hid[:, 1, m, :], sq[:, j, :], hid[:, 0, m, :].bitcast(F32),
                                           ALU.subtract).then_inc(hid_ready, 1)
                split_los(S_M2[k][half] + 2, end)

            pool.wait_ge(blk_evac, B_OUT[1] + KC)
            pool.dma_start(ptab[:, :], a["ptab"]).then_inc(s_ptab, 16)
            pool.memset(relb, NEG).then_inc(negb_set, 1)
            pool.wait_ge(negb_set, 1)
            pool.dma_start(relb[0:NBK, :], a["relb"]).then_inc(s_tab, 16)
            for dst, name in ATT_TILES:
                pool.dma_start(dst, a[name]).then_inc(s_tab, 16)
            pool.wait_ge(s_ptab, 16)
            pool.memset(h1s[0][:, :, NCMP:NCMP + 1], 0.0)
            pool.memset(h1s[1][:, :, NCMP:NCMP + 1], 0.0).then_inc(s_const, 1)
            pool.memset(bdn, NEG).then_inc(negb_set, 1)
            x_los(0)
            mlp_los(0, 0, S_M1[0][1] + 2)
            mlp_los(0, 1, S_KV + 2)

            def load_rows(b):
                for pg in range(NPG):
                    page = pool.value_load(ptab[0:1, b * NPG + pg:b * NPG + pg + 1], min_val=0, max_val=NPHYS - 1)
                    pool.dma_start(ct[b % 2][:, pg, :], a["cmp"][page, :, :]).then_inc(ct_loaded[b % 2], 16)

            pool.wait_ge(cbt_ready, 1)
            pool.wait_ge(bt_stored, 16)
            pool.dma_start(cw1, a["cw1"]).then_inc(s_cw1, 16)
            pool.wait_ge(rows_loaded, 16 * NH)
            pool.wait_ge(s_tab, 16 * N_ATT)
            pool.wait_ge(negb_set, 2)
            pool.tensor_copy(bd[:, 0:PAST - P], nr[:, 0:1].to_broadcast([P, PAST - P]))
            pool.tensor_copy(bd[:, PAST - P:PAST], nr[:, 0:P])
            pool.tensor_copy(bdw[:, NS:PAST - P], nr[:, 0:1].to_broadcast([P, PAST - P - NS]))
            pool.tensor_copy(bdw[:, PAST - P:PAST], nr[:, 0:P])
            pool.tensor_tensor(bdw[:, 0:NS], nr[:, 0:1].to_broadcast([P, NS]), wmask, ALU.add)
            c0 = FARC * CS - (PAST - P - CL + 1)
            pool.tensor_copy(bdc[:, 0:FARC], nr[:, 0:1].to_broadcast([P, FARC]))
            pool.tensor_copy(bdc[:, FARC:NCMP], nr[:, c0:c0 + CS * (NCMP - FARC - 1) + 1:CS])
            pool.tensor_copy(bdn.rearrange("p (b k) -> p b k", k=72)[:, :, 0:NS],
                             nr[:, P:P + NS].unsqueeze(1).to_broadcast([P, NB, NS])).then_inc(bd_ready, 1)
            x_los(1)
            split_los(S_KV + 2, S_Q + 2)
            pool.wait_ge(blk_evac, B_Q)
            pool.dma_start(a["o_kv"], kvT).then_inc(outs, 16)
            split_los(S_Q + 2, S_O + 2)
            pool.wait_ge(blk_evac, B_O)
            load_rows(0)
            load_rows(1)
            pool.wait_ge(zx_ready, 8)
            for half in range(2):
                d = (1 - half) * HD
                v = tp[d:d + HD].rearrange("p k g j c -> p (k g) (j c)") \
                    .rearrange("p (m h) x -> p m h x", h=2)[:, :, half, :]
                pool.dma_start(v, zx[half * HD:half * HD + HD, :, :]).then_inc(tp_loaded, 16)
            for b in range(2, NB):
                pool.wait_ge(ch_done[1], b - 1)
                load_rows(b)
            pool.wait_ge(gate_ready, 1)
            pool.dma_start(a["gscr"], gates[0:ND, 4, :]).then_inc(gate_stored, 16)
            pool.wait_ge(gate_stored, 16)
            for h in range(NH):
                src = bass.AP(a["gscr"].tensor, 3 * h, [[3 * NH, NS], [NS * 3 * NH, NB], [1, 3]])
                pool.dma_start(gn[h * NS:(h + 1) * NS, :, :], src).then_inc(gn_loaded, 16)
            for qt, g, br, u in ITEMS:
                n = (qt + 1) * P
                pool.wait_ge(wt_ready, u + 1)
                pool.tensor_tensor(Pb[u % 2][:, :, 0:n], Pb[u % 2][:, :, 0:n],
                                   wt[:, u % 2, :].unsqueeze(2).to_broadcast([P, GR, n]), ALU.mult
                                   ).then_inc(pn_ready, 1)
            for b in range(NB):
                pool.wait_ge(kv_loaded[b % 2], 80 * (b // 2 + 1))
                pool.dma_start(a["o_win"][b, :, :, :], wkv[b % 2]).then_inc(win_stored[b % 2], 16)
            pool.wait_ge(win_stored[0], 16 * NB // 2)
            pool.wait_ge(win_stored[1], 16 * NB // 2)
            pool.wait_ge(outs, 64)
            split_los(S_O + 2, S_M1[1][0] + 2)
            x_los(2)
            mlp_los(1, 0, S_M1[1][1] + 2)
            mlp_los(1, 1, N_SLOTS)
            pool.wait_ge(x_ready, 4 * KC)
            pool.dma_start(a["o_y"], xT).then_inc(x_out, 16)
            pool.wait_ge(x_out, 16)

        @block.scalar
        def _(act):
            for dst, name in PARAM_TILES[:1]:
                act.dma_start(dst, a[name]).then_inc(s_dtw, 16)
            for q in range(4):
                act.dma_start(xT[:, 2 * q:2 * q + 2, :], a["x"][:, 2 * q:2 * q + 2, :]).then_inc(s_x, 16)
            for dst, name in PARAM_TILES[1:]:
                act.dma_start(dst, a[name]).then_inc(s_par, 16)

            def split_hi(s, i=None):
                j = s % NSLOT
                act.wait_ge(w_ready[j], at_step(16 * (s // NSLOT) + 16, i, 16))
                if s >= NSLOT:
                    act.wait_ge(w_used, at_step(s + 1 - NSLOT, i, NSLOT))
                act.activation(split[:, j, 0, :], ring[:, j, :], ACT.Copy).then_inc(w_hi, 1)

            def split_his(first, last):
                with act.Fori(0, (last - first) // NSLOT) as i:
                    for j in range(NSLOT):
                        split_hi(first + j, i)

            split_hi(0)
            for m in range(KC):
                act.wait_ge(s_x, 16 * 4)
                act.activation(xs[:, 0, m, :], xT[:, m, :], ACT.Copy).then_inc(x_hi, 1)
            split_hi(1)

            act.wait_ge(s_par, 16 * (N_PARAMS - 1))
            act.wait_ge(dt_done, 1)
            act.activation(dtT[:, 0:NP_TOK], bX[0:MH, :], ACT.Identity, bias=dtb[:, 0:1])
            link(act, "act", act.activation(dtT[:, NP_TOK:T], bM[0:MH, 0:ND], ACT.Identity, bias=dtb[:, 0:1]))
            link(act, "act", act.activation(dw[0], dtT, ACT.Abs))
            act.activation(dw[1], dw[0], ACT.Exp, scale=-1.0)
            act.activation(dtb[:, 1:2], dtb[:, 1:2], ACT.Exp).then_inc(dt_abs, 1)

            def evac(blk):
                g, j = divmod(blk, GB)
                par = blk % 2
                act.wait_ge(w_used, blk + 1)
                if j < XB:
                    x = g * XB + j
                    if x >= 2:
                        act.wait_ge(conv_done, x - 1)
                    else:
                        act.wait_ge(dt_done, 1)
                        act.wait_ge(x_split, KC)
                    act.activation(raw_new(x % 2)[:, :, 0:3], cst[:, x, :, :], ACT.Copy)
                    act.activation(raw[x % 2][:, 3:3 + HT], dense[:, 2 * par, 0:HT], ACT.Copy)
                    act.activation(raw[x % 2][:, 3 + HT:3 + NP_TOK], dense[:, 2 * par + 1, 0:NPB], ACT.Copy)
                    act.activation(raw_new(x % 2)[:, :, 3:3 + NS], by_seq(dense[:, 2 * par + 1, NPB:HT]), ACT.Copy
                                   ).then_inc(blk_evac, 1)
                else:
                    m = g * 4 + j - XB
                    act.activation(halves(y[:, m, :]), dense_out(par), ACT.Silu).then_inc(blk_evac, 1)

            def conv_silu(blk):
                g, j = divmod(blk, GB)
                if j >= XB:
                    return
                x = g * XB + j
                act.wait_ge(conv_done, x + 1)
                if g >= 2:
                    act.wait_ge(y_gated, (g - 1) * NT)
                act.activation(xbc[g % 2][:, j, :], acc[x % 2], ACT.Silu).then_inc(xbc_ready, 1)

            act.wait_ge(dec_sum, 1)
            act.activation(dec_tok[:, 0:4, :].rearrange("p c h -> p (c h)"), bS[:, 0, 0:4 * MH], ACT.Exp)
            act.activation(dec_tok[0:ND, 4, :], bS[0:ND, 0, 4 * MH:NT * MH], ACT.Exp)
            act.activation(tot.rearrange("p c h -> p (c h)"), bS[:, 0, NT * MH:(NT + 4) * MH], ACT.Exp)
            act.activation(totd.rearrange("p b h -> p (b h)"), bS[:, 1, 0:NB * MH], ACT.Exp
                           ).then_inc(dec_ready, 1)
            for blk in range(GB):
                evac(blk)
                split_hi(blk + 2)
                if blk:
                    conv_silu(blk - 1)

            def y_hi_of(m):
                act.wait_ge(y_normed, m + 1)
                act.activation(y_hi[:, m, :], y[:, m, :], ACT.Copy).then_inc(y_his, 1)

            for g, c, n in TILES:
                L = width(c)
                for half in range(2):
                    act.wait_ge(seg_done, 2 * n + half + 1)
                    act.activation(Lm[0:L, half * 4:half * 4 + 4, 0:L],
                                   bS[0:L, half, 0:4 * L].rearrange("p (h l) -> p h l", h=4),
                                   ACT.Exp).then_inc(lm_ready, 1)
                act.wait_ge(ac_done, n + 1)
                act.activation(E[:, 0:4 * L], bX[:, 0:4 * L], ACT.Exp).then_inc(e_ready, 1)
                if g == MG - 1 and c < 2:
                    act.wait_ge(w_used, SL_IN)
                    for m in ((0, 1, 2, 3, 4, 5, 6, 7), (8, 9, 10, 11))[c]:
                        y_hi_of(m)
                for s_ in filler(g, c):
                    if g + 1 < MG:
                        evac(s_)
                    split_hi(s_ + 2)
                    if g + 1 < MG:
                        conv_silu(s_ - 1)
                if c == 4:
                    act.wait_ge(y_gated, n + 1)
                    for m in range(4):
                        if g * 4 + m >= 2:
                            act.wait_ge(nsq_used, g * 4 + m - 1)
                        act.activation(sq[:, m % 2, :], y[:, g * 4 + m, :], ACT.Square).then_inc(nsq_ready, 1)
                    act.wait_ge(nvar_ready, g + 1)
                    act.activation(row[:, :], row[:, :], ACT.Sqrt).then_inc(nroot_ready, 1)

            for m in range(12, 16):
                y_hi_of(m)
            split_his(S_OUT[1] + 2, S_M1[0][0] + 2)

            def layer_norm(k):
                act.wait_ge(ln_mean, k + 1)
                act.activation(halves(row[:, :]), stat, ACT.Copy).then_inc(ln_mu, 1)
                for m in range(KC):
                    act.wait_ge(ln_cent, k * KC + m + 1)
                    if m >= 2:
                        act.wait_ge(ln_used, k * KC + m - 1)
                    act.activation(sq[:, m % 2, :], xT[:, m, :], ACT.Square).then_inc(ln_sq, 1)
                act.wait_ge(ln_var, k + 1)
                act.activation(row[:, :], row[:, :], ACT.Sqrt).then_inc(ln_root, 1)
                for m in range(KC):
                    act.wait_ge(ln_scaled, k * KC + m + 1)
                    ends = dict(bias=lnb[:, k, m:m + 1], scale=lng[:, k, m:m + 1])
                    if k < 3:
                        act.activation(xs[:, 0, m, :], xT[:, m, :], ACT.Identity, **ends)
                    act.activation(xT[:, m, :], xT[:, m, :], ACT.Identity, **ends).then_inc(x_ready, 1)

            def mlp_his(k, half, end):
                with act.Fori(0, H1 // NSLOT) as i:
                    for j in range(NSLOT):
                        split_hi(S_M1[k][half] + 2 + j, i)
                        act.wait_ge(hid_sq, i * NSLOT + ((2 * k + half) * H1 + j + 1))
                        act.activation(hid[:, 0, i * NSLOT + j, :], sq[:, j, :], ACT.Copy).then_inc(hid_hi, 1)
                split_his(S_M2[k][half] + 2, end)

            layer_norm(0)
            mlp_his(0, 0, S_M1[0][1] + 2)
            mlp_his(0, 1, S_KV + 2)
            layer_norm(1)
            split_his(S_KV + 2, S_O + 2)

            act.wait_ge(blk_evac, B_O)
            for own in range(2):
                for m in range(4):
                    kv, gp = divmod(m, 2)
                    for half in range(2):
                        ps = slice(half * HD, half * HD + HD)
                        src = kvT[ps, m, 0:NP_TOK].rearrange("p (c j h) -> p j h c", c=NCMP, h=2)
                        if own:
                            act.activation(tp[ps, kv, 2 * gp + half, :, :], src[:, :, half, :], ACT.Copy
                                           ).then_inc(tp_ready, 1)
                        else:
                            act.activation(zx[ps, m, :].rearrange("p (j c) -> p j c", j=8),
                                           src[:, :, 1 - half, :], ACT.Copy).then_inc(zx_ready, 1)

            act.wait_ge(gate_done, 1)
            act.activation(gates[:, 0:4, :].rearrange("p c h -> p (c h)"), bM[:, 0:4 * 3 * NH], ACT.Exp, scale=-1.0)
            act.activation(gates[0:ND, 4, :], bM[0:ND, 4 * 3 * NH:5 * 3 * NH], ACT.Exp, scale=-1.0
                           ).then_inc(gate_exp, 1)

            for s_ in range(NB + 1):
                for kv in range(2):
                    act.wait_ge(ch_sum[kv], s_ + 1)
                    act.activation(hs[kv].rearrange("p g c -> p (g c)"), hs[kv].rearrange("p g c -> p (g c)"),
                                   ACT.Silu, bias=hpe[:, kv:kv + 1]).then_inc(ch_ready[kv], 1)

            def copy_probs(t):
                if t % 2 == 0:
                    act.wait_ge(tp_done[0], t // 2 + 1)
                    if t >= 4:
                        act.wait_ge(pv_done, t - 3)
                    n = tile_rows(t)
                    act.activation(PT[t % 4][0:n, :], bX[0:n, :], ACT.Copy).then_inc(pt_ready[0], 1)

            def exps(u):
                qt, g, br, _ = ITEMS[u]
                n = (qt + 1) * P
                act.wait_ge(mx_ready, u + 1)
                for r in range(GR):
                    last = act.activation(Pb[u % 2][:, r, 0:n], Pb[u % 2][:, r, 0:n], ACT.Exp,
                                          bias=nmx[:, u % 2, r:r + 1], accum_out=sm[:, u % 2, r:r + 1])
                last.then_inc(ex_done, 1)

            exps(0)
            for u in range(len(ITEMS)):
                qt, g, br, _ = ITEMS[u]
                if u % 8 == 0:
                    act.wait_ge(pc_sub, qt + 1)
                    act.activation(Pc.rearrange("p h c -> p (h c)"), Pc.rearrange("p h c -> p (h c)"), ACT.Exp
                                   ).then_inc(pc_exp, 1)
                if u + 1 < len(ITEMS):
                    exps(u + 1)
                for t in range(prob_tiles(u)[0], prob_tiles(u)[1]):
                    copy_probs(t)
                if u % 4 == 3:
                    act.wait_ge(pv_done, prob_tiles(u)[1])
                    gp = g // 2
                    act.activation(qT[:, gp * GR:(gp + 1) * GR, tok(qt)],
                                   bDn[:, (u // 4) % 2, :].rearrange("p (r q) -> p r q", r=GR), ACT.Copy
                                   ).then_inc(o_ready, 1)

            def new_exps(b):
                act.wait_ge(nmx_ready, b + 1)
                p_ = Pd[b % 2]
                W = PAST + ND
                for i, (lo, hi) in enumerate(((0, W), (W, 2 * W), (2 * W, 2 * W + NCMP))):
                    last = act.activation(p_[:, lo:hi], p_[:, lo:hi], ACT.Exp, bias=dnm[:, i:i + 1],
                                          accum_out=dsm[:, i:i + 1])
                last.then_inc(nex_done, 1)

            new_exps(0)
            for b in range(NB):
                act.wait_ge(ntp_done, b + 1)
                act.activation(PTd[:, 0:PAST], bX[:, :], ACT.Copy)
                act.activation(PTs[0:ND, 0:2 * P], bDn[0:ND, 1, 0:2 * P], ACT.Copy)
                act.activation(PTs[0:NCMP, 2 * P:3 * P], bDn[0:NCMP, 1, 2 * P:3 * P], ACT.Copy
                               ).then_inc(npt_act, 1)
                if b + 1 < NB:
                    new_exps(b + 1)
                act.wait_ge(no_done, b + 1)
                act.activation(qT[:, :, NP_TOK + b * NS:NP_TOK + (b + 1) * NS],
                               bDn[:, 0, 0:2 * GR * NS].rearrange("p (m i) -> p m i", i=NS), ACT.Copy
                               ).then_inc(no_ready, 1)
            act.wait_ge(no_ready, NB)
            act.wait_ge(o_ready, len(ITEMS) // 4)
            for i in range(2):
                act.wait_ge(win_stored[i], 16 * NB // 2)
            for m in range(KC):
                act.activation(xs[:, 0, m, :], qT[:, m, :], ACT.Copy).then_inc(o_hi, 1)
            split_his(S_O + 2, S_M1[1][0] + 2)
            layer_norm(2)
            mlp_his(1, 0, S_M1[1][1] + 2)
            mlp_his(1, 1, N_SLOTS)
            layer_norm(3)

        @block.tensor
        def _(pe):
            def dense_block(blk, s0, nsl, hi, lo, i=None, step=0, ready=None):
                par = blk % 2
                if blk >= 2:
                    pe.wait_ge(blk_evac, at_step(blk - 1, i, 2))
                for s in range(s0, s0 + nsl):
                    j = s % NSLOT
                    pe.wait_ge(w_split, at_step(s + 1, i, step))
                    for k in range(KC):
                        kk = (s - s0) * KC + k
                        if ready:
                            pe.wait_ge(ready[0], max(ready[1] + kk + 1, 1))
                        cols = slice(k * P, (k + 1) * P)
                        for t, (w, v) in enumerate(((0, hi), (0, lo), (1, hi))):
                            for h_ in range(2):
                                mm = pe.matmul(dense[:, 2 * par + h_, 0:HT], split[:, j, w, cols],
                                               v[:, kk, h_ * HT:(h_ + 1) * HT],
                                               start=kk == 0 and t == 0, stop=kk == nsl * KC - 1 and t == 2)
                    mm.then_inc(w_used, 1)

            def projection(b0, s0, blocks, nsl, hi, lo, ready=None):
                for j in range(2):
                    dense_block(b0 + j, s0 + j * nsl, nsl, hi, lo, ready=ready if j == 0 else None)
                with pe.Fori(1, blocks // 2) as i:
                    for j in range(2):
                        dense_block(b0 + j, s0 + j * nsl, nsl, hi, lo, i, 2 * nsl)

            x_h, x_l = xs[:, 0], xs[:, 1]

            def in_block(blk, ready=None):
                dense_block(blk, blk, 1, x_h, x_l, ready=ready)

            pe.wait_ge(s_dtw, 16)
            pe.wait_ge(s_x, 16 * 4)
            for k in range(KC):
                ends = dict(start=k == 0, stop=k == KC - 1)
                pe.matmul(bX[0:MH, :], dtw[:, k, :], xT[:, k, 0:NP_TOK], **ends)
                mm = pe.matmul(bM[0:MH, 0:ND], dtw[:, k, :], xT[:, k, NP_TOK:T], **ends)
            mm.then_inc(dt_done, 1)
            in_block(0, (x_split, 0))
            pe.wait_ge(s_par, 16 * (N_PARAMS - 1))
            pe.wait_ge(dt_ready, 1)
            for c in range(NT):
                L = width(c)
                pe.transpose(bX[0:L, c * 64:c * 64 + MH], dtT[:, tok(c)], ident[0:MH, 0:MH])
                mm = pe.transpose(bX[0:L, c * 64 + MH:c * 64 + 64], aT[:, tok(c)], ident[0:MH, 0:MH])
            mm.then_inc(dt_tr, 1)
            in_block(1)
            pe.wait_ge(am_ready, 1)
            pe.wait_ge(s_const, 1)
            for c in range(NT):
                L = width(c)
                pe.matmul(bS[0:L, 0, c * MH:(c + 1) * MH], low[0:L, c // 4, 0:L], a_tok[0:L, c, :],
                          start=True, stop=True)
            for c in range(4):
                pe.matmul(bS[:, 0, (NT + c) * MH:(NT + c + 1) * MH], ones[:, :], a_tok[:, c, :],
                          start=True, stop=True)
            pe.matmul(bS[:, 1, 0:NB * MH], ones[0:ND, :], am.rearrange("p b h -> p (b h)"),
                      start=True, stop=True).then_inc(dec_sum, 1)
            for blk in range(2, GB):
                in_block(blk)

            def inner_sums(g, c, n):
                L = width(c)
                xg = xbc[g % 2]
                if c == 0:
                    pe.wait_ge(xbc_ready, (g + 1) * XB)
                if n:
                    pe.wait_ge(y_read, n)
                    pe.wait_ge(st_ready, states_before(n - 1) + (NB if (n - 1) % NT == 4 else 1))
                else:
                    pe.wait_ge(dec_ready, 1)
                if c == 0 and g:
                    pe.wait_ge(nvar_ready, g)
                for j in range(4):
                    pe.transpose(bX[0:L, j * P:(j + 1) * P], xg[:, j, tok(c)], ident[:, :])
                pe.transpose(bM[0:L, 0:P], xg[:, 4, tok(c)], ident[:, :])
                pe.matmul(bM[0:L, P:P + L], xg[:, 4, tok(c)], xg[:, 5, tok(c)], start=True, stop=True
                          ).then_inc(tr_done, 1)
                pe.wait_ge(ah_ready, n + 1)
                for h in range(HPG):
                    mm = pe.matmul(bS[0:L, h // 4, (h % 4) * L:(h % 4 + 1) * L], AH[0:L, h, 0:L],
                                   triu[0:L, c // 4, 0:L], start=True, stop=True)
                    if h % 4 == 3:
                        mm.then_inc(seg_done, 1)
                pe.wait_ge(xdt_ready, n + 1)
                for j in range(4):
                    mm = pe.matmul(bX[:, j * L:(j + 1) * L],
                                   AR[0:L, j * P:(j + 1) * P],
                                   triu[0:L, c // 4, 0:L], start=True, stop=True)
                mm.then_inc(ac_done, 1)

            def outer_sums(g, c, n):
                L = width(c)
                xg = xbc[g % 2]
                pe.wait_ge(m_ready, n + 1)
                for h in range(HPG):
                    p0 = (h % 2) * MP
                    mm = pe.matmul(bS[p0:p0 + MP, 0, (h // 2) * L:(h // 2 + 1) * L],
                                   xdt[0:L, h * MP:(h + 1) * MP], Lm[0:L, h, 0:L], start=True, stop=True)
                if 1 <= c < 4:
                    pe.wait_ge(st_ready, states_before(n))
                    for j in range(4):
                        mm = pe.matmul(bS[:, 1, j * L:(j + 1) * L], st[:, g, j * P:(j + 1) * P],
                                       xg[:, 5, tok(c)], start=True, stop=True)
                if c == 4:
                    pe.wait_ge(sd_loaded, 16 * (g + 1))
                    for b in range(NB):
                        for j in range(4):
                            mm = pe.matmul(bS[:, 1, j * L + b * NS:j * L + (b + 1) * NS],
                                           sdec[:, b, j * P:(j + 1) * P],
                                           xg[:, 5, NP_TOK + b * NS:NP_TOK + (b + 1) * NS],
                                           start=True, stop=True)
                mm.then_inc(y_done, 1)
                pe.wait_ge(xdec_ready, n + 1)
                pe.wait_ge(e_ready, n + 1)
                if c < 4:
                    pe.wait_ge(btok_ready, n + 1)
                    pe.matmul(bX[:, :], Btok[0:L, :], xdec[0:L, :], start=True, stop=True).then_inc(sst_done, 1)
                else:
                    pe.wait_ge(bm_ready, g + 1)
                    for b in range(NB):
                        if b >= 2:
                            pe.wait_ge(st_ready, states_before(n) + b - 1)
                        pe.matmul((bX, bM)[b % 2][:, :], Bm[:, b, :], xdec[0:L, :], start=True, stop=True
                                  ).then_inc(sst_done, 1)

            for g, c, n in TILES:
                inner_sums(g, c, n)
                for s_ in filler(g, c):
                    if s_ % 2:
                        outer_sums(g, c, n)
                    if g + 1 < MG:
                        in_block(s_)
                    else:
                        dense_block(B_OUT[0] + s_ - S_OUT[0], s_, 1, y_hi, y_lo,
                                    ready=(y_split, 0) if s_ == S_OUT[0] else None)
                if not filler(g, c):
                    outer_sums(g, c, n)
                if c == 4:
                    pe.wait_ge(y_gated, n + 1)
                    pe.wait_ge(st_ready, states_before(n) + NB)
                    for m in range(4):
                        pe.wait_ge(nsq_ready, g * 4 + m + 1)
                        for h_ in range(2):
                            mm = pe.matmul(stat[:, h_, :], ones[:, :], sq[:, m % 2, h_ * HT:(h_ + 1) * HT],
                                           start=m == 0, stop=m == 3)
                        mm.then_inc(nsq_used, 1)

            pe.wait_ge(y_split, 12)
            projection(B_OUT[1], S_OUT[1], KC, 1, y_hi[:, 8:16], y_lo[:, 8:16], (y_split_last, -4))

            def layer_norm(k, blocks):
                if k == 1:
                    pe.wait_ge(cbt_ready, 1)
                pe.wait_ge(blk_evac, blocks)
                for m in range(KC):
                    for h_ in range(2):
                        mm = pe.matmul(stat[:, h_, :], onesd[:, :], xT[:, m, h_ * HT:(h_ + 1) * HT],
                                       start=m == 0, stop=m == KC - 1)
                mm.then_inc(ln_mean, 1)
                pe.wait_ge(ln_mu, k + 1)
                for m in range(KC):
                    pe.wait_ge(ln_sq, k * KC + m + 1)
                    for h_ in range(2):
                        mm = pe.matmul(stat[:, h_, :], onesd[:, :], sq[:, m % 2, h_ * HT:(h_ + 1) * HT],
                                       start=m == 0, stop=m == KC - 1)
                    mm.then_inc(ln_used, 1)

            def bias_tables():
                pe.wait_ge(s_tab, 16 * N_ATT)
                pe.wait_ge(ln_var, 1)
                for i, (bank, lo) in enumerate(((bS[:, 0, :], 0), (bS[:, 1, :], 512), (bX[:, :], 1024))):
                    n = min(512, XN - lo)
                    pe.matmul(bank[0:NH, 0:n], relb[:, :], eb[:, lo:lo + n], start=True, stop=True
                              ).then_inc(bt_done, 1)
                pe.wait_ge(bt_ready, 1)
                for i in range(NSIG):
                    o_ = i * NH
                    x0 = X0 + CB0 - CS * i
                    mm = pe.matmul(bS[:, o_ // 512, o_ % 512:o_ % 512 + NH], ef[:, x0:x0 + P], relb[:, :],
                                   start=True, stop=True)
                mm.then_inc(cbt_done, 1)

            def mlp(k):
                for half in range(2):
                    projection(B_M1[k][half], S_M1[k][half], H1, 1, x_h, x_l,
                               (x_split, (1, 3)[k] * KC) if half == 0 else None)
                    if k == 0 and half == 0:
                        bias_tables()
                    projection(B_M2[k][half], S_M2[k][half], KC, 2, hid[:, 0], hid[:, 1],
                               (hid_ready, (2 * k + half) * H1))

            layer_norm(0, B_OUT[1] + KC)
            mlp(0)
            layer_norm(1, B_M2[0][1] + KC)

            projection(B_KV, S_KV, SL_KV, 1, x_h, x_l, (x_split, 2 * KC))
            projection(B_Q, S_Q, SL_Q, 1, x_h, x_l)
            pe.wait_ge(x_ready, 2 * KC)
            for c in range(NT):
                for k in range(KC):
                    mm = pe.matmul(bM[0:width(c), c * 48:(c + 1) * 48], xT[:, k, tok(c)], gw[:, k, :],
                                   start=k == 0, stop=k == KC - 1)
            mm.then_inc(gate_done, 1)
            pe.wait_ge(blk_evac, B_Q)
            for c in range(NT):
                if c >= 2:
                    pe.wait_ge(vt_ready, c - 1)
                for j, m in enumerate((6, 7, 10, 11)):
                    mm = pe.transpose(bS[0:width(c), c % 2, j * P:(j + 1) * P], kvT[:, m, tok(c)], ident[:, :])
                mm.then_inc(vt_done, 1)

            pe.wait_ge(s_const, 2)
            pe.wait_ge(s_cw1, 16)
            for kv in range(2):
                for i in range(16):
                    mm = pe.matmul(bX[:, kv:kv + 1], cw1[:, kv, i // 8, i % 8, :], cpe[:, kv, i // 8, i % 8:i % 8 + 1],
                                   start=i == 0, stop=i == 15)
            mm.then_inc(pe_done, 1)
            pe.wait_ge(vt_ready, NT)

            def hidden(s_):
                if s_ < NB:
                    pe.wait_ge(ct_loaded[s_ % 2], 16 * NPG * (s_ // 2 + 1))
                else:
                    pe.wait_ge(tp_loaded, 32)
                    pe.wait_ge(tp_ready, 8)
                for kv in range(2):
                    if s_:
                        pe.wait_ge(ch_sum[kv], s_)
                    for r in range(2):
                        for j in range(8):
                            if s_ < NB:
                                rows = ct[s_ % 2].rearrange("p g (k j x) -> p g k j x", k=2, j=8)[:, :, kv, j, :]
                            else:
                                rows = tp[:, kv, :, j, :]
                            mm = pe.matmul(bS[:, kv, r * P:(r + 1) * P], cw1[:, kv, r, j, :], rows,
                                           start=j == 0, stop=j == 7)
                    mm.then_inc(ch_done[kv], 1)

            def compressed(s_):
                pe.wait_ge(hpe_ready, 1)
                if s_:
                    pe.wait_ge(cc_ready, s_)
                else:
                    pe.wait_ge(gate_ready, 1)
                pe.wait_ge(ch_ready[0], s_ + 1)
                for half in range(2):
                    pe.matmul(bX[half * HD:half * HD + HD, 0:2 * NCMP], cw2[:, 0, :], hs[0][:, half::2, :],
                              start=True, stop=True)
                pe.wait_ge(ch_ready[1], s_ + 1)
                for g in range(NKV):
                    mm = pe.matmul(bM[0:NCMP, g * HD:(g + 1) * HD], hs[1][:, g, :], cw2[:, 1, :],
                                   start=True, stop=True)
                mm.then_inc(cc_done, 1)

            hidden(0)
            for s_ in range(NB + 1):
                if s_ < NB:
                    hidden(s_ + 1)
                compressed(s_)

            def scores(u):
                qt, g, br, _ = ITEMS[u]
                h_ = half_of(g)
                for r in range(GR):
                    if u:
                        pe.wait_ge(sc_read, 4 * (u - 1) + r + 1)
                    pe.matmul(SB[r][:, 0:(qt + 1) * P], qT[h_, (g // 2) * GR + r, tok(qt)],
                              kvT[h_, 4 * (br + 1) + g // 2, 0:(qt + 1) * P], start=True, stop=True
                              ).then_inc(sc_done, 1)

            def compressed_scores(qt):
                if qt:
                    pe.wait_ge(pt_ready[0], (prob_tiles(8 * qt - 1)[1] + 1) // 2)
                    pe.wait_ge(pt_ready[1], prob_tiles(8 * qt - 1)[1] // 2)
                for h in range(NH):
                    g, r = divmod(h, GR)
                    c0 = ((g // 2) * GR + r) * NCMP
                    mm = pe.matmul((bX, bM)[g % 2][:, c0:c0 + NCMP], qT[half_of(g), (g // 2) * GR + r, tok(qt)],
                                   kc[half_of(g), NB, g // 2, :], start=True, stop=True)
                mm.then_inc(pcs_done, 1)

            pe.wait_ge(cc_ready, NB + 1)
            pe.wait_ge(blk_evac, B_O)
            compressed_scores(0)
            scores(0)
            for u, (qt, g, br, _) in enumerate(ITEMS):
                if u % 8 == 0 and qt:
                    compressed_scores(qt)
                if u + 1 < len(ITEMS):
                    scores(u + 1)
                o_bank = bDn[half_of(g), (u // 4) % 2, :]
                if u % 4 == 0 and u >= 8:
                    pe.wait_ge(o_ready, u // 4 - 1)
                t0, t1 = prob_tiles(u)
                if br == 0:
                    pe.wait_ge(pc_ready, qt + 1)
                if u % 8 == 0:
                    pe.wait_ge(pc_sub, qt + 1)

                def transposes(t):
                    bank = (bX, bM)[t % 2]
                    if t >= 2:
                        pe.wait_ge(pt_ready[t % 2], t // 2)
                    for r in range(GR):
                        if br == 0 and t == t0:
                            mm = pe.transpose(bank[0:NCMP, r * P:(r + 1) * P], Pc[:, g * GR + r, :], ident[:, :])
                        else:
                            kt = t - t0 - (br == 0)
                            mm = pe.transpose(bank[:, r * P:(r + 1) * P], Pb[u % 2][:, r, kt * P:(kt + 1) * P],
                                              ident[:, :])
                    mm.then_inc(tp_done[t % 2], 1)

                def values(t):
                    pe.wait_ge(pt_ready[t % 2], t // 2 + 1)
                    if br == 0 and t == t0:
                        pe.matmul(o_bank, vc[:, NB, g, :], PT[t % 4][0:NCMP, :], start=True, stop=False
                                  ).then_inc(pv_done, 1)
                    else:
                        kt = t - t0 - (br == 0)
                        mm = pe.matmul(o_bank, Vt[:, kt, br, g, :], PT[t % 4][:, :], start=False,
                                       stop=br == 1 and kt == qt)
                        mm.then_inc(pv_done, 1)

                for t in range(t0, t1):
                    if t == t0 + (br == 0):
                        pe.wait_ge(pn_ready, u + 1)
                    transposes(t)
                    if t > t0:
                        values(t - 1)
                values(t1 - 1)
            def new_scores(b):
                pe.wait_ge(kv_loaded[b % 2], 80 * (b // 2 + 1))
                if b:
                    pe.wait_ge(nsc_read, b)
                for g in range(NKV):
                    h_, rows, gp = half_of(g), slice(32 * g, 32 * g + 32), g // 2
                    q = qn[h_, gp, b, :]
                    ks = slice(gp * P, (gp + 1) * P)
                    pe.matmul(bD[0][rows, :], q, skv[b % 2][h_, :, ks], start=True, stop=True)
                    pe.matmul(bD[1][rows, :], q, wkv[b % 2][h_, :, ks], start=True, stop=True)
                    for br in range(2):
                        pe.matmul(bS[rows, 0, br * ND:(br + 1) * ND], q, kvT[h_, 4 * (br + 1) + gp, NP_TOK:T],
                                  start=True, stop=True)
                    mm = pe.matmul(bS[rows, 0, 2 * ND:2 * ND + NCMP], q, kc[h_, b, gp, :], start=True, stop=True)
                mm.then_inc(nsc_done, 1)

            pe.wait_ge(sc_read, GR * len(ITEMS))
            pe.wait_ge(o_ready, len(ITEMS) // 4)
            W = PAST + ND
            new_scores(0)
            for b in range(NB):
                if b + 1 < NB:
                    new_scores(b + 1)
                p_ = Pd[b % 2]
                pe.wait_ge(npn_ready, b + 1)
                for pg in range(NPG):
                    cols = slice(pg * P, (pg + 1) * P)
                    pe.transpose(bX[:, cols], p_[:, cols], ident[:, :])
                    pe.transpose(bM[:, cols], p_[:, W + pg * P:W + (pg + 1) * P], ident[:, :])
                for br in range(2):
                    pe.transpose(bDn[0:ND, 1, br * P:(br + 1) * P], p_[:, br * W + PAST:(br + 1) * W], ident[:, :])
                pe.transpose(bDn[0:NCMP, 1, 2 * P:3 * P], p_[:, 2 * W:2 * W + NCMP], ident[:, :]).then_inc(ntp_done, 1)
                pe.wait_ge(npt_act, b + 1)
                pe.wait_ge(npt_dve, b + 1)
                if b:
                    pe.wait_ge(no_ready, b)
                for g in range(NKV):
                    o_ = bDn[half_of(g), 0, (g // 2) * 32:(g // 2) * 32 + 32]
                    rows = slice(32 * g, 32 * g + 32)
                    vs = slice(256 + g * HD, 256 + (g + 1) * HD)
                    for pg in range(NPG):
                        k0 = pg * P + 32 * g
                        pe.matmul(o_, skv[b % 2][:, pg, vs], PTd[:, k0:k0 + 32], start=pg == 0, stop=False)
                        pe.matmul(o_, wkv[b % 2][:, pg, vs], PTd[:, PAST + k0:PAST + k0 + 32], start=False, stop=False)
                    for br in range(2):
                        pe.matmul(o_, Vt[0:ND, 4, br, g, :], PTs[0:ND, br * P + 32 * g:br * P + 32 * g + 32],
                                  start=False, stop=False)
                    mm = pe.matmul(o_, vc[:, b, g, :], PTs[0:NCMP, 2 * P + 32 * g:2 * P + 32 * g + 32],
                                   start=False, stop=True)
                mm.then_inc(no_done, 1)

            projection(B_O, S_O, SL_O, 1, x_h, x_l, (o_split, 0))
            layer_norm(2, B_O + KC)
            mlp(1)
            layer_norm(3, B_M2[1][1] + KC)

        @block.vector
        def _(dve):
            for m in range(KC):
                dve.wait_ge(x_hi, m + 1)
                dve.tensor_tensor(xs[:, 1, m, :], xT[:, m, :], xs[:, 0, m, :].bitcast(F32), ALU.subtract
                                  ).then_inc(x_split, 1)
            dve.wait_ge(dt_abs, 1)
            link(dve, "dve", dve.tensor_scalar(dw[2], dw[1], 2.0, None, ALU.add))
            link(dve, "dve", dve.reciprocal(dw[0], dw[2]))
            link(dve, "dve", dve.tensor_tensor(dw[0], dw[0], dw[1], ALU.mult))
            link(dve, "dve", dve.tensor_tensor(dw[1], dw[0], dw[0], ALU.mult))
            link(dve, "dve", dve.tensor_scalar(dw[2], dw[1], 1.0 / 17, None, ALU.mult))
            for power in (15, 13, 11, 9, 7, 5, 3):
                link(dve, "dve", dve.scalar_tensor_tensor(dw[2], dw[2], 1.0 / power, dw[1], ALU.add, ALU.mult))
            link(dve, "dve", dve.scalar_tensor_tensor(dw[2], dw[2], 1.0, dw[0], ALU.add, ALU.mult))
            dve.tensor_scalar(dw[2], dw[2], 2.0, None, ALU.mult)
            link(dve, "dve", dve.tensor_scalar(dw[3], dtT, 0.0, None, ALU.max))
            link(dve, "dve", dve.tensor_tensor(dtT, dw[2], dw[3], ALU.add))
            dve.tensor_scalar(aT, dtT, dtb[:, 1:2], -1.0, ALU.mult, ALU.mult).then_inc(dt_ready, 1)
            dve.wait_ge(dt_tr, 1)
            tr = bX[:, 0:NT * 64].rearrange("p (c k h) -> p c k h", c=NT, k=2)
            dve.tensor_copy(dt_tok[:, 0:4, :], tr[:, 0:4, 0, :])
            dve.tensor_copy(dt_tok[0:ND, 4, :], tr[0:ND, 4, 0, :])
            dve.tensor_copy(a_tok[:, 0:4, :], tr[:, 0:4, 1, :])
            dve.tensor_copy(a_tok[0:ND, 4, :], tr[0:ND, 4, 1, :]).then_inc(dt_tok_ready, 1)

            def conv(blk):
                g, j = divmod(blk, GB)
                if j >= XB:
                    return
                x = g * XB + j
                r, rn, o = raw[x % 2], raw_new(x % 2), acc[x % 2]
                on = by_seq(o[:, NP_TOK:T])
                dve.wait_ge(blk_evac, blk + 1)
                if x >= 2:
                    dve.wait_ge(xbc_ready, x - 1)
                dve.tensor_copy(lastp[:, x, :], r[:, NP_TOK:NP_TOK + 3])
                dve.tensor_copy(lastd[:, x, :, :], rn[:, :, NS:NS + 3])
                dve.tensor_scalar(o[:, 0:NP_TOK], r[:, 0:NP_TOK], cw[:, x, 0:1], cb[:, x:x + 1],
                                  ALU.mult, ALU.add)
                last = dve.tensor_scalar(on, rn[:, :, 0:NS], cw[:, x, 0:1], cb[:, x:x + 1], ALU.mult, ALU.add)
                for k in range(1, CONV):
                    link(dve, "dve", last)
                    dve.scalar_tensor_tensor(o[:, 0:NP_TOK], r[:, k:k + NP_TOK], cw[:, x, k:k + 1],
                                             o[:, 0:NP_TOK], ALU.mult, ALU.add)
                    last = dve.scalar_tensor_tensor(on, rn[:, :, k:k + NS], cw[:, x, k:k + 1], on,
                                                    ALU.mult, ALU.add)
                last.then_inc(conv_done, 1)

            def residual(blk, m, alpha, slots_used, i=None, step=0):
                dve.wait_ge(w_used, at_step(slots_used, i, step))
                xm = halves(xT[:, at_step(m, i, 2), :])
                dve.scalar_tensor_tensor(xm, xm, alpha, dense_out(blk % 2), ALU.mult, ALU.add
                                         ).then_inc(blk_evac, 1)

            dve.wait_ge(raw_zeroed, 1)
            for blk in range(GB):
                conv(blk)
            for g, c, n in TILES:
                L = width(c)
                xg = xbc[g % 2]
                gh = slice(g * HPG, (g + 1) * HPG)
                dve.wait_ge(tr_done, n + 1)
                dve.tensor_tensor(heads(xdt[0:L, :], MP), heads(bX[0:L, :], MP),
                                  over_heads(dt_tok[0:L, c, gh], L, MP), ALU.mult).then_inc(xdt_ready, 1)
                dve.tensor_copy(Btok[0:L, :], bM[0:L, 0:P]).then_inc(btok_ready, 1)
                dve.tensor_tensor(Gm[0:L, 0:L], bM[0:L, P:P + L], triu[0:L, c // 4, 0:L], ALU.mult
                                  ).then_inc(g_masked, 1)
                dve.wait_ge(g_masked, n + 1)
                dve.wait_ge(lm_ready, 2 * n + 2)
                dve.tensor_tensor(Lm[0:L, :, 0:L], Lm[0:L, :, 0:L],
                                  Gm[0:L, 0:L].unsqueeze(1).to_broadcast([L, HPG, L]), ALU.mult
                                  ).then_inc(m_ready, 1)
                if g + 1 < MG:
                    conv(filler(g, c)[0])
                elif c:
                    dve.wait_ge(x_back, 16)
                    residual(B_OUT[0], 2 * c - 2, ALPHA, filler(g, c)[0] + 1)
                dve.wait_ge(y_done, n + 1)
                dve.wait_ge(blk_evac, (g + 1) * GB)
                own = bS[:, 0, 0:4 * L]
                yv = yt[:, 0:4 * L]
                if c:
                    dve.wait_ge(e_ready, n + 1)
                    link(dve, "dve", dve.tensor_tensor(yv, bS[:, 1, 0:4 * L], E[:, 0:4 * L], ALU.mult))
                    dve.tensor_tensor(yv, yv, own, ALU.add).then_inc(y_read, 1)
                else:
                    dve.tensor_copy(yv, own).then_inc(y_read, 1)
                dve.wait_ge(y_read, n + 1)
                for j in range(4):
                    last = dve.scalar_tensor_tensor(yt[:, j * L:(j + 1) * L], xg[:, j, tok(c)],
                                                    dsk[:, g * 4 + j:g * 4 + j + 1], yt[:, j * L:(j + 1) * L],
                                                    ALU.mult, ALU.add)
                link(dve, "dve", last)
                yg = y[:, g * 4:g * 4 + 4, tok(c)]
                dve.tensor_tensor(yg, yg, yv.rearrange("p (j l) -> p j l", j=4), ALU.mult).then_inc(y_gated, 1)
                if c == 0:
                    dve.wait_ge(sst_done, states_before(n) + 1)
                    dve.tensor_copy(st[:, g, :], bX[:, :]).then_inc(st_ready, 1)
                elif c < 4:
                    dve.wait_ge(sst_done, states_before(n) + 1)
                    dve.wait_ge(stmp_ready, g * (3 + NB) + c)
                    dve.tensor_tensor(st[:, g, :], bX[:, :], tmp[0], ALU.add).then_inc(st_ready, 1)
                else:
                    for b in range(NB):
                        dve.wait_ge(sst_done, states_before(n) + b + 1)
                        dve.wait_ge(stmp_ready, g * (3 + NB) + 3 + b + 1)
                        dve.tensor_tensor(sdec[:, b, :], (bX, bM)[b % 2][:, :], tmp[b % 2], ALU.add
                                          ).then_inc(st_ready, 1)
                if g + 1 < MG:
                    conv(filler(g, c)[1])
                elif c:
                    residual(B_OUT[0] + 1, 2 * c - 1, ALPHA, filler(g, c)[1] + 1)
                if c == 4:
                    dve.wait_ge(nsq_used, (g + 1) * 4)
                    dve.tensor_scalar(halves(row[:, :]), stat, 1.0 / 512, RMS_EPS, ALU.mult, ALU.add
                                      ).then_inc(nvar_ready, 1)
                    dve.wait_ge(nroot_ready, g + 1)
                    link(dve, "dve", dve.reciprocal(row[:, :], row[:, :]))
                    for m in range(4 * g, 4 * g + 4):
                        dve.scalar_tensor_tensor(y[:, m, :], y[:, m, :], nw[:, m:m + 1], row[:, :],
                                                 ALU.mult, ALU.mult).then_inc(y_normed, 1)
            for m in range(12, 16):
                dve.wait_ge(y_his, m + 1)
                dve.tensor_tensor(y_lo[:, m, :], y[:, m, :], y_hi[:, m, :].bitcast(F32), ALU.subtract
                                  ).then_inc(y_split_last, 1)

            def residuals(b0, s0, nsl, alpha):
                with dve.Fori(0, KC // 2) as i:
                    for j in range(2):
                        residual(b0 + j, j, alpha, s0 + (j + 1) * nsl, i, 2 * nsl)

            def layer_norm(k):
                dve.wait_ge(ln_mu, k + 1)
                for m in range(KC):
                    dve.tensor_tensor(xT[:, m, :], xT[:, m, :], row[:, :], ALU.subtract).then_inc(ln_cent, 1)
                dve.wait_ge(ln_used, (k + 1) * KC)
                dve.tensor_scalar(halves(row[:, :]), stat, LN_EPS, None, ALU.add).then_inc(ln_var, 1)
                dve.wait_ge(ln_root, k + 1)
                link(dve, "dve", dve.reciprocal(row[:, :], row[:, :]))
                for m in range(KC):
                    dve.tensor_tensor(xT[:, m, :], xT[:, m, :], row[:, :], ALU.mult).then_inc(ln_scaled, 1)

            def hidden_block(k, half, j, i=None):
                h = sq[:, j, :]
                h0 = (2 * k + half) * H1
                dve.wait_ge(w_used, at_step(S_M1[k][half] + j + 1, i, 2))
                if h0 + j >= 2 or i is not None:
                    dve.wait_ge(hid_ready, at_step(h0 + j - 1, i, 2))
                dve.tensor_scalar(halves(h), dense_out(j), 0.0, None, ALU.max).then_inc(blk_evac, 1)
                dve.wait_ge(blk_evac, at_step(B_M1[k][half] + j + 1, i, 2))
                dve.tensor_tensor(h, h, h, ALU.mult).then_inc(hid_sq, 1)

            def mlp_hidden(k, half):
                for j in range(2):
                    hidden_block(k, half, j)
                with dve.Fori(1, H1 // 2) as i:
                    for j in range(2):
                        hidden_block(k, half, j, i)

            residuals(B_OUT[1], S_OUT[1], 1, 1.0)
            layer_norm(0)
            mlp_hidden(0, 0)
            dve.wait_ge(bt_done, 3)
            dve.tensor_copy(bt[:, 0:512], bS[0:NH, 0, :])
            dve.tensor_copy(bt[:, 512:1024], bS[0:NH, 1, :])
            dve.tensor_copy(bt[:, 1024:XN], bX[0:NH, 0:XN - 1024]).then_inc(bt_ready, 1)
            dve.wait_ge(cbt_done, 1)
            flat = cbt.rearrange("p s h -> p (s h)")
            dve.tensor_copy(flat[:, 0:512], bS[:, 0, :])
            dve.tensor_copy(flat[:, 512:NSIG * NH], bS[:, 1, 0:NSIG * NH - 512]).then_inc(cbt_ready, 1)
            residuals(B_M2[0][0], S_M2[0][0], 2, ALPHA)
            mlp_hidden(0, 1)
            residuals(B_M2[0][1], S_M2[0][1], 2, 1.0)
            layer_norm(1)

            with dve.Fori(0, SL_KV // 2) as i:
                for j in range(2):
                    dve.wait_ge(w_used, i * 2 + (S_KV + j + 1))
                    dve.tensor_scalar(halves(kvT[:, i * 2 + j, :]), dense_out(j), 1.0, None, ALU.mult
                                      ).then_inc(blk_evac, 1)
            for m in range(SL_Q):
                dve.wait_ge(w_used, S_Q + m + 1)
                dve.tensor_scalar(halves(qT[:, m, :]), dense_out(m % 2), SCALE, None, ALU.mult)
                dve.tensor_scalar(qn[:, m // GR, :, (m % GR) * NS:(m % GR + 1) * NS],
                                  by_seq(dense[:, 2 * (m % 2) + 1, NPB:HT]), SCALE, None,
                                  ALU.mult).then_inc(blk_evac, 1)
            dve.wait_ge(gate_exp, 1)
            dve.tensor_scalar(gates[:, 0:4, :], gates[:, 0:4, :], 1.0, None, ALU.add)
            link(dve, "dve", dve.tensor_scalar(gates[0:ND, 4, :], gates[0:ND, 4, :], 1.0, None, ALU.add))
            dve.reciprocal(gates[:, 0:4, :], gates[:, 0:4, :])
            dve.reciprocal(gates[0:ND, 4, :], gates[0:ND, 4, :]).then_inc(gate_ready, 1)
            for c in range(NT):
                dve.wait_ge(vt_done, c + 1)
                dve.tensor_copy(Vt[0:width(c), c, :, :, :].rearrange("p b g d -> p (b g d)"),
                                bS[0:width(c), c % 2, :]).then_inc(vt_ready, 1)
            dve.wait_ge(pe_done, 1)
            dve.tensor_copy(hpe, bX[:, 0:2]).then_inc(hpe_ready, 1)

            def keep_compressed(s_):
                dve.wait_ge(cc_done, s_ + 1)
                dve.tensor_copy(kc[:, s_, :, :].rearrange("p g c -> p (g c)"), bX[:, 0:2 * NCMP])
                dve.tensor_copy(vc[:, s_, :, :].rearrange("p g d -> p (g d)"), bM[0:NCMP, 0:NKV * HD]
                                ).then_inc(cc_ready, 1)

            for s_ in range(NB + 1):
                if s_:
                    keep_compressed(s_ - 1)
                for kv in range(2):
                    dve.wait_ge(ch_done[kv], s_ + 1)
                    if s_ < NB:
                        part = [bS[:, kv, r * P:(r + 1) * P].rearrange("p (t g c) -> p g t c", t=NPG, g=NKV)
                                for r in range(2)]
                        view = lambda v: v.rearrange("p g (t c) -> p g t c", t=NPG)
                    else:
                        part = [bS[:, kv, r * P:(r + 1) * P].rearrange("p (g c) -> p g c", g=NKV)
                                for r in range(2)]
                        view = lambda v: v
                    link(dve, "dve", dve.tensor_copy(view(h1s[kv][:, :, 0:NCMP]), part[1]))
                    dve.tensor_tensor(view(hs[kv]), part[0], view(h1s[kv][:, :, 1:NCMP + 1]), ALU.add
                                      ).then_inc(ch_sum[kv], 1)
            keep_compressed(NB)

            def compressed_probs(qt):
                hc = "p h c -> p (h c)"
                dve.wait_ge(pcs_done, qt + 1)
                s0 = 24 - 8 * qt
                for g in range(NKV):
                    h0 = g * GR
                    src = (bX, bM)[g % 2][:, (g // 2) * P:(g // 2 + 1) * P].rearrange("p (h c) -> p h c", h=GR)
                    last = dve.tensor_tensor(Pc[:, h0:h0 + GR, :], src, cbt[:, s0:s0 + NCMP, h0:h0 + GR]
                                             .rearrange("p s h -> p h s"), ALU.add)
                link(dve, "dve", last)
                link(dve, "dve", dve.tensor_reduce(cmx, Pc, AX.X, ALU.max))
                dve.tensor_tensor(Pc, Pc, cmx.unsqueeze(2).to_broadcast([P, NH, NCMP]), ALU.subtract
                                  ).then_inc(pc_sub, 1)
                dve.wait_ge(pc_exp, qt + 1)
                link(dve, "dve", dve.tensor_reduce(csm, Pc, AX.X, ALU.add))
                link(dve, "dve", dve.reciprocal(csm, csm))
                link(dve, "dve", dve.scalar_tensor_tensor(csm, csm, cvalid[:, qt:qt + 1], gates[:, qt, 0:46:3],
                                                          ALU.mult, ALU.mult))
                dve.tensor_tensor(Pc, Pc, csm.unsqueeze(2).to_broadcast([P, NH, NCMP]), ALU.mult
                                  ).then_inc(pc_ready, 1)

            def maxima(u):
                qt, g, br, _ = ITEMS[u]
                n = (qt + 1) * P
                far = max(n - RB, 0)
                if u >= 2:
                    dve.wait_ge(pv_done, prob_tiles(u - 2)[1])
                for r in range(GR):
                    h = g * GR + r
                    dve.wait_ge(sc_done, GR * u + r + 1)
                    if far:
                        dve.tensor_tensor_reduce(Pb[u % 2][:, r, 0:far], SB[r][:, 0:far],
                                                 Rs[:, h, 0:1].to_broadcast([P, far]), 1.0, -3.0e38,
                                                 ALU.add, ALU.max, mx[:, 0, r:r + 1])
                    last = dve.tensor_tensor_reduce(Pb[u % 2][:, r, far:n], SB[r][:, far:n],
                                                    Rs[:, h, RB - (n - far):RB], 1.0, -3.0e38,
                                                    ALU.add, ALU.max, mx[:, 1, r:r + 1])
                    last.then_inc(sc_read, 1)
                dve.wait_ge(sc_read, GR * (u + 1))
                if far:
                    link(dve, "dve", dve.tensor_tensor(mx[:, 1, :], mx[:, 0, :], mx[:, 1, :], ALU.max))
                dve.tensor_scalar(nmx[:, u % 2, :], mx[:, 1, :], -1.0, None, ALU.mult).then_inc(mx_ready, 1)

            dve.wait_ge(strips_loaded, 16)
            maxima(0)
            for u, (qt, g, br, _) in enumerate(ITEMS):
                if u % 8 == 0:
                    compressed_probs(qt)
                dve.wait_ge(ex_done, u + 1)
                link(dve, "dve", dve.reciprocal(wt[:, u % 2, :], sm[:, u % 2, :]))
                g0 = 12 * g + 1 + br
                dve.tensor_tensor(wt[:, u % 2, :], wt[:, u % 2, :], gates[:, qt, g0:g0 + 10:3], ALU.mult
                                  ).then_inc(wt_ready, 1)
                if u + 1 < len(ITEMS):
                    maxima(u + 1)
                for t in range(*prob_tiles(u)):
                    if t % 2:
                        dve.wait_ge(tp_done[1], t // 2 + 1)
                        if t >= 4:
                            dve.wait_ge(pv_done, t - 3)
                        rows = tile_rows(t)
                        dve.tensor_copy(PT[t % 4][0:rows, :], bM[0:rows, :]).then_inc(pt_ready[1], 1)

            W = PAST + ND

            def new_maxima(b):
                dve.wait_ge(nsc_done, b + 1)
                if b >= 2:
                    dve.wait_ge(ntp_done, b - 1)
                p_ = Pd[b % 2]
                new = bdn[:, b * ND:(b + 1) * ND]
                for i, (lo, hi, bank, bias) in enumerate((
                        (0, PAST, bD[0][:, :], bd), (W, W + PAST, bD[1][:, :], bdw),
                        (2 * W, 2 * W + NCMP, bS[:, 0, 2 * ND:2 * ND + NCMP], bdc),
                        (PAST, W, bS[:, 0, 0:ND], new), (W + PAST, 2 * W, bS[:, 0, ND:2 * ND], new))):
                    last = dve.tensor_tensor_reduce(p_[:, lo:hi], bank, bias, 1.0, -3.0e38, ALU.add, ALU.max,
                                                    dmx[:, i:i + 1])
                last.then_inc(nsc_read, 1)
                dve.wait_ge(nsc_read, b + 1)
                link(dve, "dve", dve.tensor_tensor(dmx[:, 0:2], dmx[:, 0:2], dmx[:, 3:5], ALU.max))
                dve.tensor_scalar(dnm, dmx[:, 0:3], -1.0, None, ALU.mult).then_inc(nmx_ready, 1)

            dve.wait_ge(bd_ready, 1)
            dve.wait_ge(gn_loaded, 16 * NH)
            new_maxima(0)
            for b in range(NB):
                dve.wait_ge(nex_done, b + 1)
                link(dve, "dve", dve.reciprocal(dwt, dsm))
                dve.tensor_tensor(dwt[:, 0:2], dwt[:, 0:2], gn[:, b, 1:3], ALU.mult)
                link(dve, "dve", dve.tensor_tensor(dwt[:, 2:3], dwt[:, 2:3], gn[:, b, 0:1], ALU.mult))
                for i, (lo, hi) in enumerate(((0, W), (W, 2 * W), (2 * W, 2 * W + NCMP))):
                    v = Pd[b % 2][:, lo:hi]
                    last = dve.tensor_scalar(v, v, dwt[:, i:i + 1], None, ALU.mult)
                last.then_inc(npn_ready, 1)
                if b + 1 < NB:
                    new_maxima(b + 1)
                dve.wait_ge(ntp_done, b + 1)
                dve.tensor_copy(PTd[:, PAST:2 * PAST], bM[:, :]).then_inc(npt_dve, 1)

            for i in range(2):
                dve.wait_ge(win_stored[i], 16 * NB // 2)
            for m in range(KC):
                dve.wait_ge(o_hi, m + 1)
                dve.tensor_tensor(xs[:, 1, m, :], qT[:, m, :], xs[:, 0, m, :].bitcast(F32), ALU.subtract
                                  ).then_inc(o_split, 1)
            residuals(B_O, S_O, 1, ALPHA)
            layer_norm(2)
            dve.wait_ge(outs, 64)
            mlp_hidden(1, 0)
            residuals(B_M2[1][0], S_M2[1][0], 2, ALPHA)
            mlp_hidden(1, 1)
            residuals(B_M2[1][1], S_M2[1][1], 2, 1.0)
            layer_norm(3)




def slots(w):
    K, M = w.shape
    v = w.reshape(K // D, KC, P, M // P, P)
    return v.transpose(3, 0, 2, 1, 4).reshape(-1, P, SLOT)


def feat(v):
    v = v.reshape(*v.shape[:-1], -1, P)
    return np.moveaxis(v, -1, 0)


def kernel(**inputs):
    import numpy as _np
    import concourse.bacc as _bacc
    from concourse import mybir as _mybir
    from concourse.bass_utils import run_bass_kernel_spmd as _run

    x = {k: _np.asarray(v) for k, v in inputs.items()}
    A = {}
    A["x"] = feat(_np.concatenate([x["x_prompt"].reshape(NP_TOK, D), x["x_sample"].reshape(ND, D)]))\
        .transpose(0, 2, 1)
    win = x["m_in_w"][0]
    z, xs, Bw, Cw, dtw = _np.split(win, [DI, 2 * DI, 2 * DI + 512, 2 * DI + 1024], axis=1)
    order = []
    for g in range(MG):
        order += [xs[:, g * 512:(g + 1) * 512], Bw[:, g * P:(g + 1) * P], Cw[:, g * P:(g + 1) * P],
                  z[:, g * 512:(g + 1) * 512]]

    def mlp_slots(layer):
        parts = []
        for half in range(2):
            cols = slice(half * DFF // 2, (half + 1) * DFF // 2)
            parts += [slots(x["mlp_w1"][layer][:, cols]), slots(x["mlp_w2"][layer][cols])]
        return parts

    A["w"] = _np.concatenate([slots(_np.concatenate(order, axis=1)), slots(x["m_out_w"][0][0:D]),
                              slots(x["m_out_w"][0][D:]), *mlp_slots(0), slots(x["kv_w"]),
                              slots(q_columns(x["q_w"][0])), slots(o_rows(x["o_w"][0])), *mlp_slots(1)])
    A["dtw"] = dtw.reshape(KC, P, MH).transpose(1, 0, 2)
    A["dtb"] = _np.stack([x["m_dt_bias"][0], x["m_a_log"][0]], axis=1)

    def conv_order(v):
        a_, b_, c_ = _np.split(v, [DI, DI + 512], axis=-1)
        parts = []
        for g in range(MG):
            parts += [a_[..., g * 512:(g + 1) * 512], b_[..., g * P:(g + 1) * P], c_[..., g * P:(g + 1) * P]]
        return feat(_np.concatenate(parts, axis=-1))

    A["cst"] = conv_order(x["state_conv"][0]).transpose(0, 3, 1, 2)
    A["cw"] = conv_order(x["m_conv_w"][0]).transpose(0, 2, 1)
    A["cb"] = conv_order(x["m_conv_b"][0])
    A["nw"] = feat(x["m_norm_w"][0])
    A["dsk"] = feat(_np.broadcast_to(x["m_d"][0][:, None], (MH, MP)).reshape(-1))
    A["lng"] = feat(x["ln_g"].reshape(4, D))
    A["lnb"] = feat(x["ln_b"].reshape(4, D))
    A["state"] = x["state_ssm"][0].transpose(0, 3, 1, 2).reshape(NB, MN, DI)
    t = _np.arange(P)
    seq = _np.arange(ND) // NS
    same = _np.zeros((P, P), bool)
    same[:ND, :ND] = seq[:, None] == seq[None, :]
    upper = t[:, None] <= t[None, :]
    A["triu"] = _np.stack([upper, upper & same], axis=1).astype(_np.float32)
    A["low"] = _np.stack([~upper, ~upper & same], axis=1).astype(_np.float32)
    A["ident"] = _np.eye(P, dtype=_np.float32)
    A["smask"] = (seq[:, None] == _np.arange(NB)[None, :]).astype(_np.float32)
    outs = {"o_pssm": (P, DI), "o_sssm": (NB, MN, DI), "o_pconv": (P, NXB, 3), "o_sconv": (P, NXB, NB, 3)}
    attention_layout(A, outs, x)

    nc = _bacc.Bacc("TRN2", target_bir_lowering=False, num_devices=1)
    dev = {}
    for name, v in A.items():
        A[name] = v = _np.ascontiguousarray(v)
        dev[name] = nc.dram_tensor("in_" + name, v.shape, _mybir.dt.from_np(v.dtype), kind="ExternalInput").ap()
    for name, shape in (("gscr", (ND, 3 * NH)), ("bscr", (NH, XN)), ("bskew", (P, NH, RW))):
        dev[name] = nc.dram_tensor(name, shape, F32, kind="Internal").ap()
    for name, shape in outs.items():
        dev[name] = nc.dram_tensor(name, shape, F32, kind="ExternalOutput").ap()
    build(nc, dev)
    r = _run(nc, [{"in_" + name: v for name, v in A.items()}], core_ids=[0]).results[0]
    return finish(r)


def q_columns(w):
    return w[:, :D].reshape(D, 2, 2, GR, HD).transpose(0, 1, 3, 2, 4).reshape(D, D)


def o_rows(w):
    return w.reshape(2, 2, GR, HD, D).transpose(0, 2, 1, 3, 4).reshape(D, D)


def kv_rows(c):
    lead = c.shape[:-4]
    k = c[..., 0, :, :].reshape(*lead, PAGE, 2, P)
    k = np.moveaxis(k, -1, -3)
    k = np.swapaxes(k, -1, -2).reshape(*lead, P, 256)
    v = c[..., 1, :, :].reshape(*lead, PAGE, 256)
    return np.concatenate([k, v], axis=-1)


def kv_rows_back(r):
    lead = r.shape[:-2]
    k = np.swapaxes(r[..., 0:256].reshape(*lead, P, 2, PAGE), -1, -2)
    k = np.moveaxis(k, -3, -1).reshape(*lead, PAGE, NKV, HD)
    v = r[..., 256:512].reshape(*lead, PAGE, NKV, HD)
    return np.stack([k, v], axis=-3)


def bucket(dist):
    n = np.maximum(dist, 16).astype(np.float64)
    large = 16 + np.floor(np.log(n / 16) / np.log(8.0) * 16 + 1e-9).astype(int)
    return np.where(dist < 0, NBK, np.where(dist < 16, np.maximum(dist, 0), np.minimum(large, NBK - 1)))


def attention_layout(A, outs, x):
    f32 = np.float32
    rows = np.arange(NBK + 1)[:, None]
    A["eb"] = (rows == bucket(Y0 - np.arange(XN))[None, :]).astype(f32)
    A["ef"] = (rows == bucket(np.arange(XN) - X0)[None, :]).astype(f32)
    A["relb"] = x["rel_bias"]
    A["gw"] = x["q_w"][0][:, D:].reshape(KC, P, 3 * NH).transpose(1, 0, 2)
    A["cw1"] = x["cmp_w1"].reshape(2, 2, 8, P, P).transpose(3, 0, 1, 2, 4)
    A["cw2"] = x["cmp_w2"].transpose(1, 0, 2)
    A["cpe"] = x["cmp_pe"].reshape(2, 2, 8, P).transpose(3, 0, 1, 2)
    q = np.arange(NP_TOK)
    A["cvalid"] = (q >= CL - 1).astype(f32).reshape(4, P).T
    i = np.arange(P) % NS
    A["wmask"] = np.where(np.arange(NS)[None, :] <= i[:, None], NEG, 0.0).astype(f32)
    A["ptab"] = x["page_table"].reshape(1, NB * NPG)
    A["sel"] = kv_rows(x["cache_sel_kv"])
    A["win"] = kv_rows(x["cache_win_kv"].reshape(NB, NPG, PAGE, 2, NKV, HD)).transpose(0, 2, 1, 3)
    A["cmp"] = x["cache_cmp_kv"].reshape(NPHYS, 8, 8, 2, 2, NKV, HD).transpose(0, 3, 6, 4, 2, 5, 1)\
        .reshape(NPHYS, P, 512)
    outs.update(o_kv=(P, 12, T), o_win=(NB, P, NPG, 512), o_y=(P, KC, T))


def finish(r):
    def tokens(v):
        return np.ascontiguousarray(np.asarray(v).transpose(2, 1, 0)).reshape(v.shape[2], -1)

    y = tokens(r["o_y"])
    kv = tokens(r["o_kv"]).reshape(T, 3, 2, NKV, HD)
    new = kv[NP_TOK:].reshape(NB, NS, 3, 2, NKV, HD)
    win = kv_rows_back(np.asarray(r["o_win"]).transpose(0, 2, 1, 3)).reshape(NB, PAST, 2, NKV, HD)
    p_ssm = np.asarray(r["o_pssm"]).reshape(MN, MH, MP).transpose(1, 2, 0)[None, None]
    s_ssm = np.asarray(r["o_sssm"]).reshape(NB, MN, MH, MP).transpose(0, 2, 3, 1)[None]

    def conv_rows(v):
        v = np.moveaxis(np.asarray(v), (1, 0), (-2, -1))
        v = v.reshape(*v.shape[:-2], MG, XB, P)
        lead = v.shape[:-3]
        return np.concatenate([v[..., 0:4, :].reshape(*lead, DI), v[..., 4, :].reshape(*lead, MG * P),
                               v[..., 5, :].reshape(*lead, MG * P)], axis=-1)

    p_conv = conv_rows(r["o_pconv"])[None, None]
    s_conv = conv_rows(r["o_sconv"])[None]
    out = (y[:NP_TOK].reshape(1, NP_TOK, D), y[NP_TOK:].reshape(NB, NS, D), p_ssm, p_conv,
           kv[None, :NP_TOK, 0], kv[None, :NP_TOK, 1], kv[None, :NP_TOK, 2],
           s_ssm, s_conv, new[:, :, 0], new[:, :, 1], np.concatenate([win[:, NS:], new[:, :, 2]], axis=1))
    return tuple(np.ascontiguousarray(v) for v in out)
```
